# Optimizing a Trainium2 kernel written in Bass

```python
import math
import jax, jax.numpy as jnp
from jax import lax
import numpy as np

D_MODEL = 2048
BATCH = 1
SEQ = 256
DEPTH = 1

LRU_WIDTH = D_MODEL
LRU_HEADS = 16
LRU_HEAD_DIM = LRU_WIDTH // LRU_HEADS
CONV_W = 4
LRU_C = 8.0
HEAD_DIM = 128
N_Q_HEADS = 16
N_KV_HEADS = 4
GQA_GROUP = N_Q_HEADS // N_KV_HEADS
WINDOW = 128
ATTN_WIDTH = N_Q_HEADS * HEAD_DIM
KV_WIDTH = N_KV_HEADS * HEAD_DIM
N_BRANCHES = 2
C_IN = 2 * LRU_WIDTH + ATTN_WIDTH + 2 * KV_WIDTH + N_BRANCHES * D_MODEL
SPLITS = tuple(np.cumsum([LRU_WIDTH, LRU_WIDTH, ATTN_WIDTH, KV_WIDTH, KV_WIDTH]).tolist())
FFN_HIDDEN = int(math.ceil(8 * D_MODEL / 3 / 256) * 256)
N_MOD = 6
EPS = 1e-6


def rms_norm(x, g):
    xf = x.astype(jnp.float32)
    inv = lax.rsqrt(jnp.mean(xf * xf, axis=-1, keepdims=True) + EPS)
    return (xf * inv).astype(x.dtype) * g

def modulate(h, shift, scale):
    return h * (1 + scale) + shift

def causal_depthwise_conv(u, w, b):
    S = u.shape[1]
    up = jnp.pad(u, ((0, 0), (CONV_W - 1, 0), (0, 0)))
    out = b
    for k in range(CONV_W):
        out = out + up[:, k:k + S, :] * w[k]
    return out

def rg_lru(u, wa, ba, wx, bx, lam):
    B, S, C = u.shape
    uh = u.reshape(B, S, LRU_HEADS, LRU_HEAD_DIM)
    r = jax.nn.sigmoid(jnp.einsum('bshi,hij->bshj', uh, wa).reshape(B, S, C) + ba)
    i = jax.nn.sigmoid(jnp.einsum('bshi,hij->bshj', uh, wx).reshape(B, S, C) + bx)
    log_a = -LRU_C * r.astype(jnp.float32) * jax.nn.softplus(-lam.astype(jnp.float32))
    a = jnp.exp(log_a)
    beta = jnp.sqrt(-jnp.expm1(2.0 * log_a))
    inp = beta * (i * u).astype(jnp.float32)

    def combine(left, right):
        a1, b1 = left
        a2, b2 = right
        return a1 * a2, a2 * b1 + b2

    _, h = lax.associative_scan(combine, (a, inp), axis=1)
    return h.astype(u.dtype)

def sliding_window_attention(q, k, v, sinks):
    B, S = q.shape[0], q.shape[1]
    nb = S // WINDOW
    qb = q.reshape(B, nb, WINDOW, N_KV_HEADS, GQA_GROUP, HEAD_DIM)
    kb = k.reshape(B, nb, WINDOW, N_KV_HEADS, HEAD_DIM)
    vb = v.reshape(B, nb, WINDOW, N_KV_HEADS, HEAD_DIM)
    pad = ((0, 0), (1, 0), (0, 0), (0, 0), (0, 0))
    kw = jnp.concatenate([jnp.pad(kb, pad)[:, :-1], kb], axis=2)
    vw = jnp.concatenate([jnp.pad(vb, pad)[:, :-1], vb], axis=2)
    s = jnp.einsum('bnqhgd,bnkhd->bnhgqk', qb, kw).astype(jnp.float32) * (HEAD_DIM ** -0.5)
    qi = jnp.arange(WINDOW)[:, None]
    kk = jnp.arange(2 * WINDOW)[None, :]
    band = (kk > qi) & (kk <= qi + WINDOW)
    blk = jnp.arange(nb)[:, None, None]
    valid = band[None] & (blk * WINDOW + kk[None] - WINDOW >= 0)
    s = jnp.where(valid[None, :, None, None], s, -jnp.inf)
    sink = sinks.astype(jnp.float32).reshape(N_KV_HEADS, GQA_GROUP)[None, None, :, :, None, None]
    m = jnp.maximum(jnp.max(s, axis=-1, keepdims=True), sink)
    p = jnp.exp(s - m)
    denom = jnp.sum(p, axis=-1, keepdims=True) + jnp.exp(sink - m)
    p = (p / denom).astype(v.dtype)
    o = jnp.einsum('bnhgqk,bnkhd->bnqhgd', p, vw)
    return o.reshape(B, S, ATTN_WIDTH)

def first_inputs(seed: int = 0) -> dict:
    key = jax.random.key(seed)
    ks = jax.random.split(key, 24)
    f32 = jnp.float32

    def nrm(k, shape, scale):
        return jax.random.normal(k, shape, f32) * scale

    a0 = jax.random.uniform(ks[11], (DEPTH, LRU_WIDTH), f32, 0.9, 0.999)
    p0 = a0 ** (1.0 / LRU_C)
    lru_lambda = jnp.log(p0) - jnp.log1p(-p0)
    return {
        "x": nrm(ks[0], (BATCH, SEQ, D_MODEL), 1.0),
        "c": nrm(ks[1], (BATCH, D_MODEL), 1.0),
        "ada_w": nrm(ks[2], (DEPTH, D_MODEL, N_MOD * D_MODEL), D_MODEL ** -0.5),
        "ada_b": nrm(ks[3], (DEPTH, N_MOD * D_MODEL), 0.01),
        "norm1_g": 1.0 + nrm(ks[4], (DEPTH, D_MODEL), 0.02),
        "w_in": nrm(ks[5], (DEPTH, D_MODEL, C_IN), D_MODEL ** -0.5),
        "b_in": nrm(ks[6], (DEPTH, C_IN), 0.01),
        "conv_w": nrm(ks[7], (DEPTH, CONV_W, LRU_WIDTH), CONV_W ** -0.5),
        "conv_b": nrm(ks[8], (DEPTH, LRU_WIDTH), 0.01),
        "lru_wa": nrm(ks[9], (DEPTH, LRU_HEADS, LRU_HEAD_DIM, LRU_HEAD_DIM), LRU_HEAD_DIM ** -0.5),
        "lru_ba": nrm(ks[10], (DEPTH, LRU_WIDTH), 0.01),
        "lru_wx": nrm(ks[12], (DEPTH, LRU_HEADS, LRU_HEAD_DIM, LRU_HEAD_DIM), LRU_HEAD_DIM ** -0.5),
        "lru_bx": nrm(ks[13], (DEPTH, LRU_WIDTH), 0.01),
        "lru_lambda": lru_lambda,
        "sinks": nrm(ks[14], (DEPTH, N_Q_HEADS), 0.5),
        "w_lru_out": nrm(ks[15], (DEPTH, LRU_WIDTH, D_MODEL), LRU_WIDTH ** -0.5),
        "w_attn_out": nrm(ks[16], (DEPTH, ATTN_WIDTH, D_MODEL), ATTN_WIDTH ** -0.5),
        "w_o": nrm(ks[17], (DEPTH, D_MODEL, D_MODEL), D_MODEL ** -0.5),
        "norm2_g": 1.0 + nrm(ks[18], (DEPTH, D_MODEL), 0.02),
        "w_ffn_in": nrm(ks[19], (DEPTH, D_MODEL, 2 * FFN_HIDDEN), D_MODEL ** -0.5),
        "w_ffn_out": nrm(ks[20], (DEPTH, FFN_HIDDEN, D_MODEL), FFN_HIDDEN ** -0.5),
        "final_g": 1.0 + nrm(ks[21], (D_MODEL,), 0.02),
    }

def first_block(x, c, ada_w, ada_b, norm1_g, w_in, b_in, conv_w, conv_b, lru_wa, lru_ba,
              lru_wx, lru_bx, lru_lambda, sinks, w_lru_out, w_attn_out, w_o, norm2_g,
              w_ffn_in, w_ffn_out, final_g):
    B, S, _ = x.shape
    c_act = jax.nn.silu(c)
    for l in range(DEPTH):
        mod = (c_act @ ada_w[l] + ada_b[l])[:, None, :]
        sh1, sc1, g1, sh2, sc2, g2 = jnp.split(mod, N_MOD, axis=-1)

        h = modulate(rms_norm(x, norm1_g[l]), sh1, sc1)
        proj = h @ w_in[l] + b_in[l]
        u, lru_gate, q, k, v, mix_gates = jnp.split(proj, SPLITS, axis=-1)

        u = causal_depthwise_conv(u, conv_w[l], conv_b[l])
        y_lru = rg_lru(u, lru_wa[l], lru_ba[l], lru_wx[l], lru_bx[l], lru_lambda[l])
        y_lru = y_lru * jax.nn.gelu(lru_gate, approximate=True)

        y_attn = sliding_window_attention(
            q.reshape(B, S, N_Q_HEADS, HEAD_DIM),
            k.reshape(B, S, N_KV_HEADS, HEAD_DIM),
            v.reshape(B, S, N_KV_HEADS, HEAD_DIM),
            sinks[l])

        gate_lru, gate_attn = jnp.split(jax.nn.sigmoid(mix_gates), N_BRANCHES, axis=-1)
        merged = gate_lru * (y_lru @ w_lru_out[l]) + gate_attn * (y_attn @ w_attn_out[l])
        x = x + g1 * (merged @ w_o[l])

        h2 = modulate(rms_norm(x, norm2_g[l]), sh2, sc2)
        gate, up = jnp.split(h2 @ w_ffn_in[l], 2, axis=-1)
        x = x + g2 * ((jax.nn.silu(gate) * up) @ w_ffn_out[l])
    return rms_norm(x, final_g)


HYENA_WIDTH = 1024
CONV_WIDTH = 3
FILTER_EMB_DIM = 33
FILTER_HIDDEN = 64
DECAY_TARGET = 1e-2
FAST_DECAY_PCT = 0.3
SLOW_DECAY_PCT = 1.5
DECAY_SHIFT = 0.05

N_HEADS = 8
QK_NOPE_DIM = 128
QK_ROPE_DIM = 64
V_HEAD_DIM = 128
Q_LORA_RANK = 512
KV_LORA_RANK = 256
ROPE_THETA = 10000.0
Q_BLOCK = 128

ATTN_WIDTH_2 = N_HEADS * V_HEAD_DIM
MIX_WIDTH = HYENA_WIDTH + ATTN_WIDTH_2
IN_PROJ_WIDTH = 3 * HYENA_WIDTH + Q_LORA_RANK + KV_LORA_RANK + QK_ROPE_DIM

D_FF = 5632
NORM_EPS = 1e-6


def _rmsnorm(x, gain):
    xf = x.astype(jnp.float32)
    y = xf * lax.rsqrt(jnp.mean(xf * xf, axis=-1, keepdims=True) + NORM_EPS)
    return (y * gain.astype(jnp.float32)).astype(x.dtype)

def _dwconv_centred(x, w, b):
    k = w.shape[0]
    half = k // 2
    s = x.shape[1]
    xp = jnp.pad(x, ((0, 0), (half, half), (0, 0)))
    return sum(xp[:, j:j + s] * w[j] for j in range(k)) + b

def _position_features(L):
    t = jnp.linspace(0.0, 1.0, L, dtype=jnp.float32)[:, None]
    bands = (FILTER_EMB_DIM - 1) // 2
    w = 2.0 * math.pi * jnp.arange(L, dtype=jnp.float32) / L
    f = jnp.linspace(1e-4, bands - 1, bands, dtype=jnp.float32)
    ang = w[:, None] * f[None, :]
    return t, jnp.concatenate([t, jnp.cos(ang), -jnp.sin(ang)], axis=-1)

def _implicit_filters(t, z, w1, b1, fr1, w2, b2, fr2, w3):
    f32 = jnp.float32
    L = t.shape[0]
    h = jnp.sin(fr1.astype(f32) * (z @ w1.astype(f32) + b1.astype(f32)))
    h = jnp.sin(fr2.astype(f32) * (h @ w2.astype(f32) + b2.astype(f32)))
    h = h @ w3.astype(f32)
    max_decay = math.log(DECAY_TARGET) / FAST_DECAY_PCT
    min_decay = math.log(DECAY_TARGET) / SLOW_DECAY_PCT
    deltas = jnp.abs(jnp.linspace(min_decay, max_decay, HYENA_WIDTH, dtype=f32))
    window = jnp.exp(-t * deltas[None, :]) + DECAY_SHIFT
    h = h.reshape(L, 2, HYENA_WIDTH) * window[:, None, :]
    h_fwd, h_bwd = h[:, 0], h[:, 1]
    return jnp.concatenate([h_fwd, jnp.zeros((1, HYENA_WIDTH), f32), h_bwd[1:][::-1]], axis=0)

def _bidir_long_conv(u, k2, bias):
    L = u.shape[1]
    n = 2 * L
    uf = jnp.fft.rfft(u.astype(jnp.float32), n=n, axis=1)
    kf = jnp.fft.rfft(k2, n=n, axis=0)
    y = jnp.fft.irfft(uf * kf[None], n=n, axis=1)[:, :L]
    return (y + u.astype(jnp.float32) * bias.astype(jnp.float32)).astype(u.dtype)

def _rope(x, cos, sin):
    x1, x2 = jnp.split(x, 2, axis=-1)
    return x * cos + jnp.concatenate([-x2, x1], axis=-1) * sin

def _mla(c_q, c_kv, k_pe, q_norm_gain, w_uq, kv_norm_gain, w_ukv, cos, sin):
    B, S, _ = c_q.shape
    dqk = QK_NOPE_DIM + QK_ROPE_DIM
    q = (_rmsnorm(c_q, q_norm_gain) @ w_uq).reshape(B, S, N_HEADS, dqk)
    q_nope, q_pe = q[..., :QK_NOPE_DIM], q[..., QK_NOPE_DIM:]
    kv = (_rmsnorm(c_kv, kv_norm_gain) @ w_ukv).reshape(B, S, N_HEADS, QK_NOPE_DIM + V_HEAD_DIM)
    k_nope, v = kv[..., :QK_NOPE_DIM], kv[..., QK_NOPE_DIM:]
    q_pe = _rope(q_pe, cos[:, None, :], sin[:, None, :])
    k_pe = _rope(k_pe, cos, sin)
    q = jnp.concatenate([q_nope, q_pe], axis=-1)
    k = jnp.concatenate([k_nope, jnp.broadcast_to(k_pe[:, :, None, :], (B, S, N_HEADS, QK_ROPE_DIM))], axis=-1)
    scale = dqk ** -0.5
    nb = S // Q_BLOCK
    qb = q.reshape(B, nb, Q_BLOCK, N_HEADS, dqk).transpose(1, 0, 2, 3, 4)

    def attend(q_blk):
        s = jnp.einsum('bqhd,bkhd->bhqk', q_blk, k).astype(jnp.float32) * scale
        p = jax.nn.softmax(s, axis=-1).astype(v.dtype)
        return jnp.einsum('bhqk,bkhd->bqhd', p, v)

    o = lax.map(attend, qb)
    return o.transpose(1, 0, 2, 3, 4).reshape(B, S, ATTN_WIDTH_2)

def second_inputs(seed: int = 0) -> dict:
    key = jax.random.key(seed)
    ks = jax.random.split(key, 32)
    f32 = jnp.float32

    def nrm(k, shape, scale):
        return jax.random.normal(k, shape, f32) * scale

    def gain(k, n):
        return 1.0 + 0.05 * jax.random.normal(k, (DEPTH, n), f32)

    return {
        "x": nrm(ks[0], (BATCH, SEQ, D_MODEL), 1.0),
        "pre_mix_gain": gain(ks[1], D_MODEL),
        "w_in": nrm(ks[2], (DEPTH, D_MODEL, IN_PROJ_WIDTH), D_MODEL ** -0.5),
        "hyena_conv_w": nrm(ks[3], (DEPTH, CONV_WIDTH, 3 * HYENA_WIDTH), CONV_WIDTH ** -0.5),
        "hyena_conv_b": nrm(ks[4], (DEPTH, 3 * HYENA_WIDTH), 0.02),
        "filt_w1": nrm(ks[5], (DEPTH, FILTER_EMB_DIM, FILTER_HIDDEN), FILTER_EMB_DIM ** -0.5),
        "filt_b1": nrm(ks[6], (DEPTH, FILTER_HIDDEN), 0.02),
        "filt_freq1": 1.0 + 0.1 * jax.random.normal(ks[7], (DEPTH, FILTER_HIDDEN), f32),
        "filt_w2": nrm(ks[8], (DEPTH, FILTER_HIDDEN, FILTER_HIDDEN), FILTER_HIDDEN ** -0.5),
        "filt_b2": nrm(ks[9], (DEPTH, FILTER_HIDDEN), 0.02),
        "filt_freq2": 1.0 + 0.1 * jax.random.normal(ks[10], (DEPTH, FILTER_HIDDEN), f32),
        "filt_w3": nrm(ks[11], (DEPTH, FILTER_HIDDEN, 2 * HYENA_WIDTH), FILTER_HIDDEN ** -0.5),
        "hyena_bias": nrm(ks[12], (DEPTH, HYENA_WIDTH), 0.5),
        "q_norm_gain": gain(ks[13], Q_LORA_RANK),
        "w_uq": nrm(ks[14], (DEPTH, Q_LORA_RANK, N_HEADS * (QK_NOPE_DIM + QK_ROPE_DIM)), Q_LORA_RANK ** -0.5),
        "kv_norm_gain": gain(ks[15], KV_LORA_RANK),
        "w_ukv": nrm(ks[16], (DEPTH, KV_LORA_RANK, N_HEADS * (QK_NOPE_DIM + V_HEAD_DIM)), KV_LORA_RANK ** -0.5),
        "hyena_out_gain": gain(ks[17], HYENA_WIDTH),
        "attn_out_gain": gain(ks[18], ATTN_WIDTH_2),
        "w_out": nrm(ks[19], (DEPTH, MIX_WIDTH, D_MODEL), MIX_WIDTH ** -0.5),
        "post_mix_gain": gain(ks[20], D_MODEL),
        "pre_ffn_gain": gain(ks[21], D_MODEL),
        "w_up": nrm(ks[22], (DEPTH, D_MODEL, 2 * D_FF), D_MODEL ** -0.5),
        "ffn_conv_w": nrm(ks[23], (DEPTH, CONV_WIDTH, D_FF), CONV_WIDTH ** -0.5),
        "ffn_conv_b": nrm(ks[24], (DEPTH, D_FF), 0.02),
        "w_down": nrm(ks[25], (DEPTH, D_FF, D_MODEL), D_FF ** -0.5),
        "post_ffn_gain": gain(ks[26], D_MODEL),
    }

def second_block(x, pre_mix_gain, w_in, hyena_conv_w, hyena_conv_b, filt_w1, filt_b1, filt_freq1,
              filt_w2, filt_b2, filt_freq2, filt_w3, hyena_bias, q_norm_gain, w_uq, kv_norm_gain,
              w_ukv, hyena_out_gain, attn_out_gain, w_out, post_mix_gain, pre_ffn_gain, w_up,
              ffn_conv_w, ffn_conv_b, w_down, post_ffn_gain):
    B, S, _ = x.shape
    pos = jnp.arange(S, dtype=jnp.float32)
    inv_freq = 1.0 / (ROPE_THETA ** (jnp.arange(0, QK_ROPE_DIM, 2, dtype=jnp.float32) / QK_ROPE_DIM))
    ang = pos[:, None] * inv_freq[None, :]
    ang = jnp.concatenate([ang, ang], axis=-1)
    cos = jnp.cos(ang).astype(x.dtype)
    sin = jnp.sin(ang).astype(x.dtype)
    t, z = _position_features(S)

    h = x
    for l in range(DEPTH):
        xn = _rmsnorm(h, pre_mix_gain[l])
        proj = xn @ w_in[l]
        o1 = 3 * HYENA_WIDTH
        o2 = o1 + Q_LORA_RANK
        o3 = o2 + KV_LORA_RANK
        xh, c_q, c_kv, k_pe = proj[..., :o1], proj[..., o1:o2], proj[..., o2:o3], proj[..., o3:]

        xh = _dwconv_centred(xh, hyena_conv_w[l], hyena_conv_b[l])
        x0 = xh[..., :HYENA_WIDTH]
        x1 = xh[..., HYENA_WIDTH:2 * HYENA_WIDTH]
        v = xh[..., 2 * HYENA_WIDTH:]
        k2 = _implicit_filters(t, z, filt_w1[l], filt_b1[l], filt_freq1[l], filt_w2[l], filt_b2[l],
                               filt_freq2[l], filt_w3[l])
        y_hyena = x0 * _bidir_long_conv(x1 * v, k2, hyena_bias[l])

        y_attn = _mla(c_q, c_kv, k_pe, q_norm_gain[l], w_uq[l], kv_norm_gain[l], w_ukv[l], cos, sin)

        mixed = jnp.concatenate([_rmsnorm(y_hyena, hyena_out_gain[l]),
                                 _rmsnorm(y_attn, attn_out_gain[l])], axis=-1) @ w_out[l]
        h = h + _rmsnorm(mixed, post_mix_gain[l])

        hn = _rmsnorm(h, pre_ffn_gain[l])
        gu = hn @ w_up[l]
        g = _dwconv_centred(gu[..., :D_FF], ffn_conv_w[l], ffn_conv_b[l])
        u = gu[..., D_FF:]
        f = (jax.nn.gelu(g, approximate=True) * u) @ w_down[l]
        h = h + _rmsnorm(f, post_ffn_gain[l])
    return h


def setup_inputs(seed=0):
    out = dict(first_inputs(seed))
    for name, value in second_inputs(seed + 1).items():
        if name != "x":
            out[name + "_2"] = value
    return out


def reference(
    x, c, ada_w, ada_b, norm1_g, w_in, b_in, conv_w, conv_b, lru_wa, lru_ba, lru_wx, lru_bx,
    lru_lambda, sinks, w_lru_out, w_attn_out, w_o, norm2_g, w_ffn_in, w_ffn_out, final_g,
    pre_mix_gain_2, w_in_2, hyena_conv_w_2, hyena_conv_b_2, filt_w1_2, filt_b1_2, filt_freq1_2,
    filt_w2_2, filt_b2_2, filt_freq2_2, filt_w3_2, hyena_bias_2, q_norm_gain_2, w_uq_2,
    kv_norm_gain_2, w_ukv_2, hyena_out_gain_2, attn_out_gain_2, w_out_2, post_mix_gain_2,
    pre_ffn_gain_2, w_up_2, ffn_conv_w_2, ffn_conv_b_2, w_down_2, post_ffn_gain_2,
):
    x = first_block(
        x, c, ada_w, ada_b, norm1_g, w_in, b_in, conv_w, conv_b, lru_wa, lru_ba, lru_wx, lru_bx,
        lru_lambda, sinks, w_lru_out, w_attn_out, w_o, norm2_g, w_ffn_in, w_ffn_out, final_g,
    )
    return second_block(
        x, pre_mix_gain_2, w_in_2, hyena_conv_w_2, hyena_conv_b_2, filt_w1_2, filt_b1_2,
        filt_freq1_2, filt_w2_2, filt_b2_2, filt_freq2_2, filt_w3_2, hyena_bias_2,
        q_norm_gain_2, w_uq_2, kv_norm_gain_2, w_ukv_2, hyena_out_gain_2, attn_out_gain_2,
        w_out_2, post_mix_gain_2, pre_ffn_gain_2, w_up_2, ffn_conv_w_2, ffn_conv_b_2, w_down_2,
        post_ffn_gain_2,
    )


_drawn_inputs = setup_inputs


def setup_inputs(seed=0):
    import zlib

    import numpy as np

    out = dict(_drawn_inputs(seed))
    spreads = {}
    factors = {'norm1_g': 3.307,
     'b_in': 3.093,
     'conv_b': 3.752,
     'lru_ba': 8.0,
     'lru_bx': 8.0,
     'sinks': 6.008,
     'norm2_g': 3.456,
     'q_norm_gain_2': 7.015,
     'ffn_conv_b_2': 5.156,
     'filt_b1_2': 2.819}
    for name, (base, spread) in spreads.items():
        noise = np.random.default_rng([zlib.crc32(name.encode()), seed]).standard_normal(out[name].shape)
        drawn = base * np.exp(spread * noise) if base else spread * noise
        out[name] = __import__('jax').numpy.asarray(drawn.astype(out[name].dtype))
    for name, factor in factors.items():
        out[name] = (out[name] * factor).astype(out[name].dtype)
    return out
```

```python
from contextlib import ExitStack

import numpy as np

import concourse.bass as bass
import concourse.mybir as mybir

F32 = mybir.dt.float32
F32R = mybir.dt.float32r
ALU = mybir.AluOpType
ACT = mybir.ActivationFunctionType
AX = mybir.AxisListType
P = 128
S = 256
DM = 2048
KT = 16
NHID = 44
CHUNKS = [range(0, 15), range(15, 30), range(30, 44)]
EPS = 1e-6
RING = 6
USLOTS = 4
SUB = 8

PV = {}
_n = 0
for _name, _w in [("norm1_g", 16), ("b_in", 88), ("conv_w", 64), ("conv_b", 16), ("lru_ba", 16), ("lru_bx", 16),
                  ("lru_lambda", 16), ("norm2_g", 16), ("final_g", 16), ("c", 16), ("ada_b", 96), ("sinks", 16),
                  ("pre_mix_gain_2", 16), ("hyena_conv_w_2", 72), ("hyena_conv_b_2", 24), ("hyena_bias_2", 8),
                  ("q_norm_gain_2", 4), ("kv_norm_gain_2", 2), ("hyena_out_gain_2", 8), ("attn_out_gain_2", 8),
                  ("post_mix_gain_2", 16), ("pre_ffn_gain_2", 16), ("ffn_conv_w_2", 132), ("ffn_conv_b_2", 44),
                  ("post_ffn_gain_2", 16), ("filt", 4)]:
    PV[_name] = _n
    _n += _w
NPV = _n


class Tok:

    def __init__(self, eng, sem=None, value=None):
        self.eng, self.sem, self.value, self.used = eng, sem, value, False


class Queues:

    def __init__(self, sems):
        self.q = {k: [] for k in sems}
        self.sems = sems

    def op(self, eng, fn, *waits):
        self.wait(eng, *waits)
        t = Tok(eng)
        self.q[eng].append((t, fn))
        return t

    def wait(self, eng, *toks):
        for t in toks:
            if t is None:
                continue
            if isinstance(t, (list, tuple)):
                self.wait(eng, *t)
                continue
            t.used = True
            self.q[eng].append((t, None))

    def count(self):
        for eng, items in self.q.items():
            n = 0
            for t, fn in items:
                if fn is not None and t.used and t.sem is None:
                    n += 1
                    t.sem, t.value = self.sems[eng], n

    def emit(self, eng, e):
        seen = {}
        for t, fn in self.q[eng]:
            if fn is None:
                if seen.get(id(t.sem), 0) < t.value:
                    e.wait_ge(t.sem, t.value)
                    seen[id(t.sem)] = t.value
            else:
                ins = fn(e)
                if t.used and t.eng != "dma":
                    ins.then_inc(t.sem, 1)


class Slot:
    def __init__(self, ap):
        self.ap, self.free = ap, []


class Turns:

    def __init__(self, aps):
        self.slots, self.n = [Slot(a) for a in aps], 0

    def next(self):
        s = self.slots[self.n % len(self.slots)]
        self.n += 1
        return s


def ring_plan():
    plan = [("ada", s, j) for s in range(4) for j in range(8)]
    w = []
    w += [("w_in", o) for o in range(16)]
    w += [("w_in", 48 + o) for o in range(8)]
    w += [("w_in", 32 + o) for o in range(16)]
    w += [("w_in", 16 + o) for o in range(16)]
    for o in range(16):
        w += [("w_in", 56 + o), ("w_lru_out", o)]
    w += [("w_in", 72 + o) for o in range(16)]
    w += [("w_attn_out", o) for o in range(16)]
    w += [("w_o", o) for o in range(16)]
    base = 0
    for c in CHUNKS:
        for h in c:
            w += [("w_ffn_in", h), ("w_ffn_in", NHID + h)]
        w += [("w_ffn_out", base + j) for j in range(len(c))]
        base += len(c)
    ada = [(s, j) for s in range(4, 12) for j in range(8)]
    for n, item in enumerate(w):
        plan.append(item)
        if (n >= 24 and n % 2 == 0 and n < 24 + 96) or (136 <= n < 136 + 16):
            if ada and not (n < 136 and ada[0][0] >= 10):
                plan.append(("ada", *ada.pop(0)))
    assert not ada
    for j in range(8):
        plan += [("w_in2", 8 + j), ("w_in2", 16 + j)]
    plan += [("w_in2", 24 + j) for j in range(8)]
    plan += [("w_in2", j) for j in range(8)]
    plan += [("w_u2", j) for j in range(6)]
    plan += [("w_out2", o) for o in range(16)]
    base = 0
    for c in CHUNKS:
        for h in c:
            plan += [("w_up2", h), ("w_up2", NHID + h)]
        plan += [("w_down2", base + j) for j in range(len(c))]
        base += len(c)
    return plan


def program(nc, d, out):
    ctx = ExitStack()
    with ctx:
        _program(nc, d, out, ctx)


def _program(nc, d, out, ctx):
    def sb(name, shape, dt=F32):
        return ctx.enter_context(nc.sbuf_tensor(name, shape, dt))

    def overlay(*views):
        made = []
        for name, shape, dt in views[:-1]:
            with nc.sbuf_tensor(name, shape, dt) as t:
                made.append(t)
        return made + [sb(*views[-1])]

    sems = {k: ctx.enter_context(nc.semaphore("s_" + k)) for k in ("pe", "act", "dve", "pool", "sp")}
    Q = Queues(sems)
    dsem = [ctx.enter_context(nc.semaphore(f"s_ring{i}")) for i in range(RING)]

    W = sb("W", [P, RING, 1024])
    WH = sb("WH", [P, USLOTS, SUB * P], F32R)
    WL = sb("WL", [P, USLOTS, SUB * P], F32R)
    XA_, XAf = overlay(("XA", [P, KT, 512], F32R), ("XAf", [P, 8192], F32))
    XA = [XA_[:, k, :] for k in range(KT)]
    XB_, XBf = overlay(("XB", [P, KT, 512], F32R), ("XBf", [P, 8192], F32))
    XB = [XB_[:, k, :] for k in range(KT)]
    RES = sb("RES", [P, KT, S])
    G1 = sb("G1", [P, KT, S])
    G2 = sb("G2", [P, 4096])
    G3 = sb("G3", [P, 4160])
    ACC = sb("ACC", [P, 2, 1024])
    PVT = sb("PVT", [P, NPV])
    IDN = sb("IDN", [P, P])
    ONE = sb("ONE", [P, P])
    MOD = sb("MOD", [P, 96])
    SM = sb("SM", [P, 128])
    SA = sb("SA", [P, S])
    INV = sb("INV", [P, S])
    EV = Turns([sb(f"EV{i}", [P, S])[:, :] for i in range(4)])
    TT = Turns([sb(f"TT{i}", [P, S])[:, :] for i in range(2)])
    PS = [ctx.enter_context(nc.psum_tensor(f"PS{i}", [P, 512], F32)) for i in range(8)]
    GB = Turns([PS[i][:, :] for i in range(3)])
    MB = Turns([PS[i][:, :] for i in range(3, 8)])

    def pv(name, j=0, n=1):
        return PVT[:, PV[name] + j:PV[name] + j + n]

    def tt(o, a, b, op, *w):
        return Q.op("dve", lambda e: e.tensor_tensor(o, a, b, op), *w)

    def stt(o, a, s, b, op0, op1, *w):
        return Q.op("dve", lambda e: e.scalar_tensor_tensor(out=o, in0=a, scalar=s, in1=b, op0=op0, op1=op1), *w)

    def ts(o, a, s1, s2, op0, op1, *w):
        if s2 is None:
            return Q.op("dve", lambda e: e.tensor_scalar(o, a, s1, None, op0), *w)
        return Q.op("dve", lambda e: e.tensor_scalar(o, a, s1, s2, op0, op1), *w)

    def vcopy(o, a, *w):
        return Q.op("dve", lambda e: e.tensor_copy(o, a), *w)

    def recip(o, a, *w):
        return Q.op("dve", lambda e: e.reciprocal(o, a), *w)

    def vmax(o, a, *w):
        return Q.op("dve", lambda e: e.tensor_reduce(o, a, AX.X, ALU.max), *w)

    def memset(o, v, *w):
        return Q.op("dve", lambda e: e.memset(o, v), *w)

    def act(o, a, f, *w, **kw):
        return Q.op("act", lambda e: e.activation(o, a, f, **kw), *w)

    def mm(o, l, r, start, stop, *w):
        return Q.op("pe", lambda e: e.matmul(o, l, r, start=start, stop=stop, skip_group_check=True), *w)

    def turn(o, a, *w):
        return Q.op("pe", lambda e: e.transpose(o, a, IDN[:, :]), *w)

    nload = [0]

    def load(o, a, *w):
        s = ctx.enter_context(nc.semaphore(f"s_load{nload[0]}"))
        nload[0] += 1
        t = Tok("dma", s, 16)
        Q.wait("sp", *w)
        Q.q["sp"].append((t, lambda e: e.dma_start(o, a).then_inc(s, 16)))
        return t

    plan = [(*item, half) for item in ring_plan() for half in range(2)]
    ring_free = [[] for _ in plan]
    ring_tok = []

    def ring_load():
        n = len(ring_tok)
        if n == len(plan):
            return
        if n >= RING:
            Q.wait("sp", *ring_free[n - RING])
        kind = plan[n]
        src = (d["ada"][kind[1], kind[2]] if kind[0] == "ada" else d[kind[0]][kind[1]])[:, kind[-1] * 1024:(kind[-1] + 1) * 1024]
        s, v, slot = dsem[n % RING], 16 * (n // RING + 1), n % RING
        t = Tok("dma", s, v)
        Q.q["sp"].append((t, lambda e: e.dma_start(W[:, slot, :], src).then_inc(s, 16)))
        ring_tok.append(t)

    at = {"ring": 0, "split": 0, "unit": -1, "sub": SUB}
    unit_tok = []
    unit_done = []
    ada_free = [[], []]
    mod_tok = {}
    c_tok = []

    def ada_tile(n):
        _, s, j, half = plan[n]
        acc, src, k = ACC[:, s % 2, :], W[:, n % RING, :], 2 * j + half
        c = SM[:, k:k + 1]
        if k == 0:
            t = ts(acc, src, c, None, ALU.mult, None, ring_tok[n], *c_tok, *ada_free[s % 2])
        else:
            t = stt(acc, src, c, acc, ALU.mult, ALU.add, ring_tok[n], ada_last[0])
        ada_last[0] = t
        ring_free[n] = [t]
        if k == 15:
            ada_pending.append((s, t))

    ada_last = [None]
    ada_pending = []

    def ada_reduce():
        while ada_pending:
            s, t = ada_pending.pop(0)
            b = MB.next()
            for i in range(8):
                m = mm(b.ap[:, i:i + 1], ACC[:, s % 2, i * P:(i + 1) * P], ONE[:, 0:1], True, True,
                       t, ones_tok[0], *b.free)
            ada_free[s % 2] = [m]
            mod_tok[s] = tt(MOD[:, 8 * s:8 * s + 8], b.ap[:, 0:8], pv("ada_b", 8 * s, 8), ALU.add, m, pv_tok[0])
            b.free = [mod_tok[s]]

    def split_next():
        while at["ring"] < len(plan) and plan[at["ring"]][0] == "ada":
            ada_tile(at["ring"])
            at["ring"] += 1
            ring_load()
        if at["ring"] == len(plan):
            return
        n, u = at["ring"], at["split"]
        src = W[:, n % RING, :]
        hi, lo = WH[:, u % USLOTS, :], WL[:, u % USLOTS, :]
        before = [unit_done[u - USLOTS]] if u >= USLOTS else []
        a = act(hi, src, ACT.Copy, ring_tok[n], *before)
        v = tt(lo, src, hi.bitcast(F32), ALU.subtract, a, *before)
        unit_tok.append(v)
        at["split"] += 1
        ring_free[n] = [v]
        at["ring"] += 1
        ring_load()

    def next_sub():
        if at["sub"] == SUB:
            at["unit"] += 1
            at["sub"] = 0
            while at["split"] < at["unit"] + USLOTS and at["ring"] < len(plan):
                split_next()
            Q.wait("pe", unit_tok[at["unit"]])
        i = at["sub"]
        at["sub"] += 1
        return at["unit"] % USLOTS, i

    def gemm(X, kts, ready):
        b = GB.next()
        n = len(kts)
        for j, kt in enumerate(kts):
            u, i = next_sub()
            hi, lo = WH[:, u, i * P:(i + 1) * P], WL[:, u, i * P:(i + 1) * P]
            mm(b.ap, hi, X[kt], j == 0, False, *(b.free if j == 0 else []), ready[kt] if ready else None)
            m = mm(b.ap[:, S:2 * S], lo, X[kt][:, 0:S], False, j == n - 1)
            if at["sub"] == SUB:
                unit_done.append(m)
        b.done = m
        pe_last[0] = m
        return b

    pe_last = [None]
    bg = []

    def background(n=1):
        for _ in range(n):
            for g in list(bg[:2]):
                if next(g, "end") == "end":
                    bg.remove(g)
            if not bg:
                return

    def drain_background():
        while bg:
            background()

    def evac(b, o, *w, bias=None, scale=None):
        t = EV.next()
        kw = {}
        if bias is not None:
            kw["bias"] = bias
        if scale is not None:
            kw["scale"] = scale
        a = act(t.ap, b.ap[:, S:2 * S], ACT.Identity, b.done, *t.free, **kw)
        if scale is None:
            v = tt(o, b.ap[:, 0:S], t.ap, ALU.add, a, *w)
        else:
            v = stt(o, b.ap[:, 0:S], scale, t.ap, ALU.mult, ALU.add, a, *w)
        b.free = [v]
        t.free = [v]
        return v

    def put_split(X, kt, src, *w):
        a = act(X[kt][:, 0:S], src, ACT.Copy, *w)
        return a, tt(X[kt][:, S:2 * S], src, X[kt][:, 0:S].bitcast(F32), ALU.subtract, a)

    class Sum:

        def __init__(self, acc, *w):
            self.acc, self.last, self.w = acc, None, list(w)

        def add(self, src, *w, scale=None):
            kw = {} if scale is None else {"scale": scale}
            if self.last is None:
                self.last = act(self.acc, src, ACT.Square, *w, *self.w, **kw)
                return self.last
            t = TT.next()
            a = act(t.ap, src, ACT.Square, *w, *t.free, **kw)
            self.last = tt(self.acc, self.acc, t.ap, ALU.add, a, self.last)
            t.free = [self.last]
            return a

        def inv(self, o, n, *w):
            b = MB.next()
            m = mm(b.ap[:, 0:S], ONE[:, :], self.acc, True, True, self.last, ones_tok[0], *b.free)
            self.done = m
            a = act(o, b.ap[:, 0:S], ACT.Sqrt, m, *w, scale=1.0 / n, bias=SM[:, 112:113])
            b.free = [a]
            return recip(o, o, a)

    pv_tok = [load(PVT[:, :], d["pv"])]
    x_view = XAf[:, 0:4096].rearrange("p (b n) -> p b n", b=2)
    id_tok = load(IDN[:, :], d["ident"])
    x_tok = load(x_view, d["x"])
    for _ in range(RING):
        ring_load()
    w3 = XBf[0:64, 4096:6144]
    zT = XBf[0:33, 6144:6400]
    w1 = XBf[0:33, 6400:6464]
    w2 = XBf[0:64, 6464:6528]
    fs = XBf[0:64, 6528:7808].rearrange("p (a n) -> p a n", a=5)
    CS = G3[:, 0:1024].rearrange("p (a b f) -> p a b f", a=2, b=2)
    win = XAf[:, 4096:8192].rearrange("p (a b n) -> p a b n", a=2, b=2)
    z_tok = [load(zT, d["zT"]), load(w1, d["filt_w1_2"]), load(w2, d["filt_w2_2"])]
    w3_tok = load(w3, d["filt_w3_2"])
    cs_tok = load(CS, d["dft"])
    win_tok = load(win, d["window"])
    lw = G2[:, :].rearrange("p (a h n) -> p a h n", a=2, h=16)
    lw_tok = load(lw, d["lru_w"])

    ones_tok = [memset(ONE[:, :], 1.0)]
    eps_tok = memset(SM[:, 112:113], EPS)
    c_tok.append(act(SM[:, 0:16], pv("c", 0, 16), ACT.Silu, pv_tok[0]))

    res_tok = [None] * KT
    for j in range(8):
        b = MB.next()
        for i in range(2):
            for tb in range(2):
                m = turn(b.ap[:, i * S + tb * P:i * S + tb * P + P],
                         x_view[:, tb, (2 * j + i) * P:(2 * j + i + 1) * P], x_tok, id_tok, *b.free)
        a = act(RES[:, 2 * j:2 * j + 2, :].rearrange("p a n -> p (a n)"), b.ap, ACT.Copy, m)
        b.free = [a]
        res_tok[2 * j] = res_tok[2 * j + 1] = a
        x_read = m
    s1 = Sum(SA[:, :])
    for kt in range(KT):
        s1.add(RES[:, kt, :], res_tok[kt])
    inv_tok = s1.inv(INV[:, :], DM, eps_tok)

    lam = pv("lru_lambda", 0, 16)
    lp = [SM[:, 16 * i:16 * i + 16] for i in range(1, 6)]
    a = act(lp[0], lam, ACT.Abs, pv_tok[0])
    a = act(lp[1], lp[0], ACT.Exp, a, scale=-1.0)
    v = ts(lp[2], lp[1], 2.0, None, ALU.add, None, a)
    v = recip(lp[2], lp[2], v)
    v = tt(lp[2], lp[1], lp[2], ALU.mult, v)
    v = tt(lp[3], lp[2], lp[2], ALU.mult, v)
    v = ts(lp[4], lp[3], 1.0 / 19, 1.0 / 17, ALU.mult, ALU.add, v)
    for k in (15, 13, 11, 9, 7, 5, 3, 1):
        v = tt(lp[4], lp[4], lp[3], ALU.mult, v)
        v = ts(lp[4], lp[4], 1.0 / k, None, ALU.add, None, v)
    v = tt(lp[4], lp[4], lp[2], ALU.mult, v)
    v1 = ts(lp[0], lam, -1.0, 0.0, ALU.mult, ALU.max, pv_tok[0], v)
    v = stt(lp[0], lp[4], 2.0, lp[0], ALU.mult, ALU.add, v1)
    SP = lp[2]
    SN = lp[3]
    v = ts(SP, lp[0], 8.0, None, ALU.mult, None, v)
    sp_tok = ts(SN, lp[0], -8.0, None, ALU.mult, None, v)

    kf_dram = nc.dram_tensor("kf", [P, 4096], F32, kind="Internal").ap()

    def sine(arg, o, t1, *w):
        mg = 12582912.0
        v = ts(t1, arg, 1.0 / (2 * np.pi), mg, ALU.mult, ALU.add, *w)
        v = ts(t1, t1, -mg, None, ALU.add, None, v)
        c1 = 6.28125
        c2 = round((2 * np.pi - c1) * 2.0**21) / 2.0**21
        c3 = float(2 * np.pi - c1 - c2)
        for c in (c1, c2, c3):
            v = stt(arg, t1, -c, arg, ALU.mult, ALU.add, v)
        v = ts(arg, arg, 3.1415925, -3.1415925, ALU.min, ALU.max, v)
        return act(o, arg, ACT.Sin, v)

    def filters():
        def layer(lhsT, rhs, k, *w):
            b = MB.next()
            m = mm(b.ap[0:64, 0:S], lhsT, rhs, True, True, *w, *b.free)
            freq, bias = (PVT[0:64, PV["filt"] + i:PV["filt"] + i + 1] for i in (k, k + 1))
            v = ts(fs[:, 0, :], b.ap[0:64, 0:S], bias, freq, ALU.add, ALU.mult, m, pv_tok[0])
            b.free = [v]
            return v

        v = layer(w1, zT, 0, *z_tok)
        yield
        a = sine(fs[:, 0, :], fs[:, 1, :], fs[:, 2, :], v)
        yield
        v = layer(w2, fs[:, 1, :], 2, a)
        yield
        a = sine(fs[:, 0, :], fs[:, 1, :], fs[:, 2, :], v)
        yield
        pq = XBf[:, 0:4096].rearrange("p (a b n) -> p a b n", a=2, b=2)
        tmp = G1[:, 0:4, :].rearrange("p (a b) n -> p a (b n)", a=2)
        toks = []
        v2 = None
        for tb in range(2):
            for ch in range(2):
                bf, bb = MB.next(), MB.next()
                mf = mm(bf.ap, fs[:, 1, tb * P:(tb + 1) * P], w3[:, ch * 512:(ch + 1) * 512], True, True, a, w3_tok, *bf.free)
                mb = mm(bb.ap, fs[:, 1, tb * P:(tb + 1) * P], w3[:, 1024 + ch * 512:1024 + (ch + 1) * 512], True, True, *bb.free)
                va = tt(tmp[:, 0, :], bf.ap, win[:, 0, tb, ch * 512:(ch + 1) * 512], ALU.mult, mf, win_tok)
                vb = tt(tmp[:, 1, :], bb.ap, win[:, 1, tb, ch * 512:(ch + 1) * 512], ALU.mult, mb)
                bf.free, bb.free = [va], [vb]
                tt(pq[:, 0, tb, ch * 512:(ch + 1) * 512], tmp[:, 0, :], tmp[:, 1, :], ALU.add, va, vb)
                v2 = tt(pq[:, 1, tb, ch * 512:(ch + 1) * 512], tmp[:, 1, :], tmp[:, 0, :], ALU.subtract)
                toks.append(v2)
                yield
        kf = G1[:, :, :].rearrange("p a n -> p (a n)").rearrange("p (a f n) -> p a f n", a=2, f=2)
        for a_ in range(2):
            for f in range(2):
                for ch in range(2):
                    b = MB.next()
                    for tb in range(2):
                        m = mm(b.ap, CS[:, a_, tb, f * P:(f + 1) * P], pq[:, a_, tb, ch * 512:(ch + 1) * 512],
                               tb == 0, tb == 1, toks[-1], cs_tok, *b.free)
                    c = act(kf[:, a_, f, ch * 512:(ch + 1) * 512], b.ap, ACT.Copy, m, toks[-1])
                    b.free = [c]
                    yield
        g1_free.append(store(kf_dram, G1[:, :, :].rearrange("p a n -> p (a n)"), c))
        xb_free.append(m)
        xa_free.append(toks[-1])
        g3_free.append(m)

    stores = []

    def store(o, a, *w):
        s = ctx.enter_context(nc.semaphore(f"s_store{len(stores)}"))
        t = Tok("dma", s, 16)
        Q.wait("sp", *w)
        Q.q["sp"].append((t, lambda e: e.dma_start(o, a).then_inc(s, 16)))
        stores.append(t)
        return t

    g1_free, xa_free, xb_free, g3_free = [], [], [], []

    flt = filters()
    for n in range(64):
        ada_tile(n)
        at["ring"] += 1
        ring_load()
        ada_reduce()
        if n % 2:
            next(flt, None)
    for _ in flt:
        pass
    SC = SM[:, 96:112]

    def scale_of(g, first):
        return stt(SC, MOD[:, first:first + 16], 1.0, pv(g, 0, 16), ALU.add, ALU.mult,
                   mod_tok[first // 8], mod_tok[first // 8 + 1])

    sc_tok = scale_of("norm1_g", 16)

    def modulated(X, shift, sc, it, *w):
        ready = []
        for kt in range(KT):
            t = TT.next()
            v = stt(t.ap, RES[:, kt, :], SC[:, kt:kt + 1], INV[:, :], ALU.mult, ALU.mult, sc, it, res_tok[kt], *t.free)
            sh = MOD[:, shift + kt:shift + kt + 1]
            a = act(X[kt][:, 0:S], t.ap, ACT.Identity, v, mod_tok[shift // 8], mod_tok[shift // 8 + 1], *w, bias=sh)
            v = stt(X[kt][:, S:2 * S], t.ap, sh, X[kt][:, 0:S].bitcast(F32), ALU.add, ALU.subtract, a)
            t.free = [v]
            ready.append(v)
        return ready

    def scaled(X, src, toks, inv, it, gain, *w, n=KT, at_=0):
        ready = []
        for kt in range(n):
            t = TT.next()
            v = stt(t.ap, src(kt), gain(kt), inv, ALU.mult, ALU.mult, it, toks[kt], *t.free)
            _, v = put_split(X, at_ + kt, t.ap, v, *w)
            t.free = [v]
            ready.append(v)
        return ready

    for _ in range(USLOTS - 1):
        split_next()
    h_ready = modulated(XA, 0, sc_tok, inv_tok, x_read, *xa_free)

    ALLK = list(range(KT))

    Y = G1
    LS = XBf[:, 0:4096].rearrange("p (a n) -> p a n", a=4)
    UP = Turns([XBf[:, 4096 + 264 * i:4096 + 264 * i + 259] for i in range(2)])
    for s in UP.slots:
        s.free = [memset(s.ap[:, 0:3], 0.0, *xb_free)]
    uc_tok = [None] * 16
    y_tok = [None] * 16
    ls_free = []

    def lru_batch(q):
        R4, I4, T4, A4 = (LS[:, i, :] for i in range(4))
        last = []
        for j in range(4):
            h = 4 * q + j
            b = MB.next()
            m = mm(b.ap[:, 0:S], lw[:, 0, h, :], Y[:, h, :], True, True, uc_tok[h], lw_tok, *b.free)
            m = mm(b.ap[:, S:2 * S], lw[:, 1, h, :], Y[:, h, :], True, True)
            a = act(R4[:, j * S:(j + 1) * S], b.ap[:, 0:S], ACT.Sigmoid, m, *ls_free, *xb_free, bias=pv("lru_ba", h))
            a = act(I4[:, j * S:(j + 1) * S], b.ap[:, S:2 * S], ACT.Sigmoid, bias=pv("lru_bx", h))
            b.free = [a]
            yield
        g2_last[0] = m
        for j in range(4):
            a = act(T4[:, j * S:(j + 1) * S], R4[:, j * S:(j + 1) * S], ACT.Tanh, a, sp_tok, scale=SP[:, 4 * q + j:4 * q + j + 1])
        for j in range(4):
            a = act(A4[:, j * S:(j + 1) * S], R4[:, j * S:(j + 1) * S], ACT.Exp, scale=SN[:, 4 * q + j:4 * q + j + 1])
        yq = Y[:, 4 * q:4 * q + 4, :].rearrange("p a n -> p (a n)")
        vi = tt(I4, I4, yq, ALU.mult, a)
        v = tt(R4, A4, A4, ALU.mult, a)
        v = stt(T4, R4, 1.0, T4, ALU.add, ALU.mult, v)
        a = act(T4, T4, ACT.Sqrt, v)
        v = tt(I4, T4, I4, ALU.mult, a, vi)
        for j in range(4):
            h = 4 * q + j
            c = slice(j * S, (j + 1) * S)
            y_tok[h] = Q.op("dve", lambda e, h=h, c=c: e.tensor_tensor_scan(Y[:, h, :], A4[:, c], I4[:, c], 0.0,
                                                                           ALU.mult, ALU.add), v, m)
        ls_free[:] = [y_tok[4 * q + 3]]
        yield

    g2_last = [None]
    for h in range(16):
        b = gemm(XA, ALLK, h_ready)
        s = UP.next()
        v = evac(b, s.ap[:, 3:3 + S], *s.free, bias=pv("b_in", h))
        w = [pv("conv_w", k * 16 + h) for k in range(4)]
        v = ts(Y[:, h, :], s.ap[:, 0:S], w[0], pv("conv_b", h), ALU.mult, ALU.add, v, *g1_free)
        for k in range(1, 4):
            v = stt(Y[:, h, :], s.ap[:, k:k + S], w[k], Y[:, h, :], ALU.mult, ALU.add, v)
        s.free = [v]
        uc_tok[h] = v
        if h % 4 == 3:
            bg.append(lru_batch(h // 4))
        background()
        ada_reduce()

    kT = G3[:, 0:1024].rearrange("p (g n) -> p g n", g=4)
    vtok = G3[:, 1024:2048].rearrange("p (b n) -> p b n", b=2)
    mask = G3[:, 2048:2304]
    mask_tok = load(mask, d["mask"], *g3_free)
    PB = Turns([G3[:, 2304 + 384 * i:2688 + 384 * i] for i in range(2)])
    PT = Turns([G3[:, 3072 + 384 * i:3456 + 384 * i] for i in range(2)])
    ST = Turns([G3[:, 3840 + 8 * i:3848 + 8 * i] for i in range(3)])
    kv_tok = {}

    def v_turn(src, s, tv, dst, key):
        b = MB.next()
        for tb in range(2):
            m = turn(b.ap[:, tb * P:(tb + 1) * P], src[:, tb * P:(tb + 1) * P], tv, id_tok, *b.free)
        s.free = [m]
        a = act(dst, b.ap[:, 0:S].rearrange("p (b n) -> p b n", b=2), ACT.Copy, m)
        b.free = [a]
        kv_tok[key] = a
        yield

    for o in range(8):
        b = gemm(XA, ALLK, None)
        g = o % 4
        if o < 4:
            kv_tok["k", g] = evac(b, kT[:, g, :], *g3_free, bias=pv("b_in", 48 + o))
        else:
            s = TT.next()
            v = evac(b, s.ap, *s.free, *g3_free, bias=pv("b_in", 48 + o))
            for _ in v_turn(s.ap, s, v, vtok[:, :, g * P:(g + 1) * P], ("v", g)):
                pass
        background()
        ada_reduce()
    QT = G2[:, :].rearrange("p (h n) -> p h n", h=16)
    q_tok = [None] * 16
    o_tok = [None] * 16
    SCALE = float(P) ** -0.5

    def head(h):
        g = h // 4
        b = MB.next()
        mm(b.ap[:, 0:P], QT[:, h, 0:P], kT[:, g, 0:P], True, True, q_tok[h], kv_tok["k", g], *b.free)
        m = mm(b.ap[:, P:P + S], QT[:, h, P:2 * P], kT[:, g, :], True, True)
        pb, st = PB.next(), ST.next()
        p = pb.ap
        v = stt(p[:, 0:P], b.ap[:, 0:P], SCALE, mask[:, P:2 * P], ALU.mult, ALU.add, m, mask_tok, *pb.free)
        v2 = stt(p[:, P:P + S], b.ap[:, P:P + S], SCALE, mask, ALU.mult, ALU.add)
        b.free = [v2]
        x = st.ap
        v = vmax(x[:, 0:1], p[:, 0:P], v, *st.free)
        v = vmax(x[:, 1:2], p[:, P:P + S], v2)
        v = ts(x[:, 0:2], x[:, 0:2], pv("sinks", h), -1.0, ALU.max, ALU.mult, v)
        a = act(p[:, 0:P], p[:, 0:P], ACT.Exp, v, bias=x[:, 0:1], accum_out=x[:, 2:3])
        a = act(p[:, P:P + S], p[:, P:P + S], ACT.Exp, bias=x[:, 1:2], accum_out=x[:, 3:4])
        a = act(x[:, 4:6], x[:, 0:2], ACT.Exp, bias=pv("sinks", h))
        v = tt(x[:, 2:4], x[:, 2:4], x[:, 4:6], ALU.add, a)
        v = recip(x[:, 2:4], x[:, 2:4], v)
        v1 = ts(p[:, 0:P], p[:, 0:P], x[:, 2:3], None, ALU.mult, None, v)
        v = ts(p[:, P:P + S], p[:, P:P + S], x[:, 3:4], None, ALU.mult, None)
        st.free = [v]
        yield
        b = MB.next()
        turn(b.ap[:, 0:P], p[:, 0:P], v, *b.free)
        turn(b.ap[:, P:2 * P], p[:, P:2 * P])
        m = turn(b.ap[:, 2 * P:3 * P], p[:, 2 * P:3 * P])
        pb.free = [m]
        pt = PT.next()
        a = act(pt.ap, b.ap[:, 0:384], ACT.Copy, m, *pt.free)
        b.free = [a]
        yield
        b = MB.next()
        v0, v1_ = vtok[:, 0, g * P:(g + 1) * P], vtok[:, 1, g * P:(g + 1) * P]
        mm(b.ap[:, 0:P], v0, pt.ap[:, 0:P], True, True, a, kv_tok["v", g], *b.free)
        mm(b.ap[:, P:2 * P], v0, pt.ap[:, P:2 * P], True, False)
        m = mm(b.ap[:, P:2 * P], v1_, pt.ap[:, 2 * P:3 * P], False, True)
        pt.free = [m]
        o_tok[h] = act(QT[:, h, :], b.ap[:, 0:S], ACT.Copy, m)
        b.free = [o_tok[h]]
        yield

    for o in range(16):
        b = gemm(XA, ALLK, None)
        assert g2_last[0] is not None
        q_tok[o] = evac(b, QT[:, o, :], g2_last[0], bias=pv("b_in", 32 + o))
        bg.append(head(o))
        if o % 2:
            background()
        else:
            background(2)
        ada_reduce()
    assert all(y_tok)

    yl_ready = [None] * KT
    lru_last = y_tok[15]
    for o in range(16):
        b = gemm(XA, ALLK, None)
        s = TT.next()
        v = evac(b, s.ap, *s.free, bias=pv("b_in", 16 + o))
        a = act(s.ap, s.ap, ACT.Gelu_apprx_tanh, v)
        v = tt(s.ap, s.ap, Y[:, o, :], ALU.mult, a, y_tok[o])
        _, v = put_split(XB, o, s.ap, v, lru_last)
        s.free = [v]
        yl_ready[o] = v
        background()
        ada_reduce()

    M = G1
    m_tok = [None] * KT
    for o in range(16):
        bm = gemm(XA, ALLK, None)
        s = TT.next()
        v = evac(bm, s.ap, *s.free, bias=pv("b_in", 56 + o))
        a = act(s.ap, s.ap, ACT.Sigmoid, v)
        bl = gemm(XB, ALLK, yl_ready)
        s2 = EV.next()
        v = evac(bl, s2.ap, *s2.free)
        m_tok[o] = tt(M[:, o, :], s.ap, s2.ap, ALU.mult, v, a, yl_ready[o])
        s.free = s2.free = [m_tok[o]]
        background()
        ada_reduce()
    drain_background()
    xb_pe = pe_last[0]

    ya_ready = [put_split(XB, h, QT[:, h, :], o_tok[h], xb_pe)[1] for h in range(16)]
    gate_tok = [None] * KT
    for o in range(16):
        b = gemm(XA, ALLK, None)
        v = evac(b, QT[:, o, :], ya_ready[o], bias=pv("b_in", 72 + o))
        gate_tok[o] = act(QT[:, o, :], QT[:, o, :], ACT.Sigmoid, v)
        ada_reduce()
    xa_pe = pe_last[0]
    mg_ready = [None] * KT
    for o in range(16):
        b = gemm(XB, ALLK, ya_ready)
        s = TT.next()
        v = evac(b, s.ap, *s.free)
        v = tt(s.ap, s.ap, QT[:, o, :], ALU.mult, v, gate_tok[o])
        v = tt(s.ap, s.ap, M[:, o, :], ALU.add, v, m_tok[o])
        _, v = put_split(XA, o, s.ap, v, xa_pe)
        s.free = [v]
        mg_ready[o] = v
        ada_reduce()

    def residual(o, b, gate, first_w):
        s = TT.next()
        v = evac(b, s.ap, *s.free, *first_w, scale=gate)
        res_tok[o] = tt(RES[:, o, :], RES[:, o, :], s.ap, ALU.add, v, res_tok[o])
        s.free = [res_tok[o]]

    s2_ = Sum(SA[:, :], s1.done)
    for o in range(16):
        b = gemm(XA, ALLK, mg_ready)
        ada_reduce()
        residual(o, b, MOD[:, 32 + o:33 + o], [mod_tok[4], mod_tok[5]])
        s2_.add(RES[:, o, :], res_tok[o])
    xa_pe = pe_last[0]
    sc_tok = scale_of("norm2_g", 64)
    inv_tok = s2_.inv(INV[:, :], DM, h_ready[-1])
    h2_ready = modulated(XA, 48, sc_tok, inv_tok, xa_pe)
    norm2_last = h2_ready[-1]

    f_last = [pe_last[0]]

    SB = G2[:, 0:S]
    sF = Sum(SA[:, :], s2_.done)
    sG = Sum(G2[:, S:2 * S])
    for ci, ch in enumerate(CHUNKS):
        f_ready = [None] * KT
        for j, hh in enumerate(ch):
            bg_ = gemm(XA, ALLK, h2_ready)
            s = TT.next()
            v = evac(bg_, s.ap, *s.free)
            a = act(s.ap, s.ap, ACT.Silu, v)
            bu = gemm(XA, ALLK, None)
            s2 = EV.next()
            v = evac(bu, s2.ap, *s2.free)
            v = tt(s.ap, s.ap, s2.ap, ALU.mult, v, a)
            s2.free = [v]
            _, v = put_split(XB, j, s.ap, v, f_last[0])
            s.free = [v]
            f_ready[j] = v
            ada_reduce()
        for o in range(16):
            b = gemm(XB, list(range(len(ch))), f_ready)
            residual(o, b, MOD[:, 80 + o:81 + o], [mod_tok[10], mod_tok[11]])
            if ci == len(CHUNKS) - 1:
                sF.add(RES[:, o, :], res_tok[o])
                sG.add(RES[:, o, :], res_tok[o], *( [gate_tok[15], mg_ready[15]] if o == 0 else []), scale=pv("final_g", o))
        f_last[0] = pe_last[0]
    xa_pe = pe_last[0]

    inv_tok = sF.inv(INV[:, :], DM, norm2_last)
    bG = MB.next()
    mG = mm(bG.ap[:, 0:S], ONE[:, :], sG.acc, True, True, sG.last, *bG.free)
    t1, t2 = G2[:, 512:768], G2[:, 768:1024]
    v = tt(t1, INV[:, :], INV[:, :], ALU.mult, inv_tok)
    v = tt(t1, bG.ap[:, 0:S], t1, ALU.mult, mG, v)
    bG.free = [v]
    a = act(t1, t1, ACT.Sqrt, v, scale=1.0 / DM, bias=SM[:, 112:113])
    inv2_tok = recip(t2, t1, a)
    xn_ready = []
    for kt in range(KT):
        res_tok[kt] = stt(RES[:, kt, :], RES[:, kt, :], pv("final_g", kt), INV[:, :], ALU.mult, ALU.mult,
                          res_tok[kt], inv_tok, sG.last)
        s = TT.next()
        v = stt(s.ap, RES[:, kt, :], pv("pre_mix_gain_2", kt), t2, ALU.mult, ALU.mult, res_tok[kt], inv2_tok, *s.free)
        _, v = put_split(XA, kt, s.ap, v, xa_pe)
        s.free = [v]
        xn_ready.append(v)

    KF = G2[:, :].rearrange("p (a f n) -> p a f n", a=2, f=2)
    kf_tok = load(G2[:, :], kf_dram, g1_free[0], xn_ready[-1])
    UT = G1[:, 0:8, :]
    X0 = G1[:, 8:16, :]
    g1_done = [mg_ready[15]]
    g3_done = [o_tok[15]]
    xb_done = [f_last[0]]
    utok = G3[:, 0:2048].rearrange("p (b n) -> p b n", b=2)
    cq = G3[:, 2048:3584].rearrange("p (a n) -> p a n", a=6)
    kpz = G3[:, 3584:4096].rearrange("p (a n) -> p a n", a=2)
    sk_acc, sk_inv = G3[:, 3584:3840], G3[:, 3840:4096]
    dft_b = XBf[:, 3072:4096].rearrange("p (a b f) -> p a b f", a=2, b=2)
    idft_b = XBf[:, 4096:5120].rearrange("p (a b f) -> p a b f", a=2, b=2)
    rope = XBf[:, 6424:6936].rearrange("p (a n) -> p a n", a=2)
    r1, r2 = XBf[:, 6936:7192], XBf[:, 7192:7448]
    prod = XBf[:, 5120:6144].rearrange("p (a n) -> p a n", a=2)
    dft_tok = load(dft_b, d["dft"], *xb_done)
    idft_tok = load(idft_b, d["idft"], *xb_done)
    rope_tok = load(rope, d["rope"], *xb_done)

    def conv_buffers(at_, *w):
        ins = Turns([at_[:, 264 * i:264 * i + 258] for i in range(3)])
        outs = Turns([at_[:, 792 + S * i:792 + S * (i + 1)] for i in range(2)])
        for s in ins.slots:
            memset(s.ap[:, 0:1], 0.0, *w)
            s.free = [memset(s.ap[:, 257:258], 0.0, *w)]
        for s in outs.slots:
            s.free = list(w)
        return ins, outs

    conv_in, conv_out = conv_buffers(XBf[:, 5120:6424], *xb_done)

    def conv3(b, ins, o, wname, bname, j, n, *w):
        s = ins.next()
        v = evac(b, s.ap[:, 1:1 + S], *s.free)
        v = ts(o, s.ap[:, 0:S], pv(wname, j), pv(bname, j), ALU.mult, ALU.add, v, *w)
        for k in (1, 2):
            v = stt(o, s.ap[:, k:k + S], pv(wname, k * n + j), o, ALU.mult, ALU.add, v)
        s.free = [v]
        return v

    ut_tok = [None] * 8
    x0_tok = [None] * 8
    utok_tok = [None] * 8

    def u_turn(j):
        b = MB.next()
        for tb in range(2):
            m = turn(b.ap[:, tb * P:(tb + 1) * P], UT[:, j, tb * P:(tb + 1) * P], ut_tok[j], *b.free)
        a = act(utok[:, :, j * P:(j + 1) * P], b.ap[:, 0:S].rearrange("p (b n) -> p b n", b=2), ACT.Copy, m, *g3_done)
        b.free = [a]
        utok_tok[j] = a
        yield

    for j in range(8):
        b = gemm(XA, ALLK, xn_ready)
        c1 = conv_out.next()
        va = conv3(b, conv_in, c1.ap, "hyena_conv_w_2", "hyena_conv_b_2", 8 + j, 24, *c1.free)
        b = gemm(XA, ALLK, None)
        vb = conv3(b, conv_in, UT[:, j, :], "hyena_conv_w_2", "hyena_conv_b_2", 16 + j, 24, *g1_done)
        ut_tok[j] = tt(UT[:, j, :], UT[:, j, :], c1.ap, ALU.mult, va, vb)
        c1.free = [ut_tok[j]]
        if j:
            background()
        bg.append(u_turn(j))

    cq_tok = [None] * 6
    sQ, sK = Sum(SA[:, :], sF.done), Sum(sk_acc, *g3_done)
    for o in range(8):
        b = gemm(XA, ALLK, None)
        if o < 6:
            cq_tok[o] = evac(b, cq[:, o, :], *g3_done)
            (sQ if o < 4 else sK).add(cq[:, o, :], cq_tok[o])
        elif o == 6:
            invq = sQ.inv(INV[:, :], 512, res_tok[15])
            invk = sK.inv(sk_inv, 256, *g3_done)
            v = evac(b, r1, *xb_done)
            ka = tt(r1, r1, rope[:, 0, :], ALU.mult, v, rope_tok)
        else:
            v = evac(b, r2, *xb_done)
            kb = tt(r2, r2, rope[:, 1, :], ALU.mult, v)
        background()
    c_ready = scaled(XB, lambda k: cq[:, k, :], cq_tok, INV[:, :], invq, lambda k: pv("q_norm_gain_2", k), *xb_done, n=4)
    c_ready += scaled(XB, lambda k: cq[:, 4 + k, :], cq_tok[4:], sk_inv, invk, lambda k: pv("kv_norm_gain_2", k),
                      *xb_done, n=2, at_=4)
    v = memset(G3[:, 3584:4096], 0.0, c_ready[-1])
    tt(kpz[0:64, 0, :], r1[0:64, :], r2[0:64, :], ALU.add, v, ka, kb)
    kp_tok = tt(kpz[64:128, 1, :], r1[64:128, :], r2[64:128, :], ALU.add)
    for j in range(8):
        b = gemm(XA, ALLK, None)
        x0_tok[j] = conv3(b, conv_in, X0[:, j, :], "hyena_conv_w_2", "hyena_conv_b_2", j, 24, *g1_done)
        background()
    drain_background()
    xa_pe = pe_last[0]

    UF = XAf[:, 0:4096].rearrange("p (a f n) -> p a f n", a=2, f=2)
    QN = XAf[:, 4096:6144].rearrange("p (h n) -> p h n", h=8)
    KN = XAf[:, 6144:8192].rearrange("p (h n) -> p h n", h=8)
    QP = G3[:, 2048:3072].rearrange("p (a n) -> p a n", a=4)
    vt2 = utok
    uf_tok = {}
    last = {"prod": x0_tok[7], "utok": None}

    def spectrum():
        for ch in range(2):
            c = slice(ch * 512, (ch + 1) * 512)
            for f in range(2):
                for a_ in range(2):
                    b = MB.next()
                    for tb in range(2):
                        m = mm(b.ap, dft_b[:, a_, tb, f * P:(f + 1) * P], utok[:, tb, c],
                               tb == 0, tb == 1, dft_tok, *utok_tok[4 * ch:4 * ch + 4], *b.free)
                    a = act(UF[:, a_, f, c], b.ap, ACT.Copy, m, xa_pe)
                    b.free = [a]
                    last["utok"] = m
                ur, vv, kr, ki = UF[:, 0, f, c], UF[:, 1, f, c], KF[:, 0, f, c], KF[:, 1, f, c]
                v1 = tt(prod[:, 0, :], ur, ki, ALU.mult, a, kf_tok, last["prod"])
                v2 = tt(prod[:, 1, :], vv, ki, ALU.mult)
                v3 = tt(ur, ur, kr, ALU.mult, v1)
                v4 = tt(vv, vv, kr, ALU.mult, v2)
                v5 = tt(ur, ur, prod[:, 1, :], ALU.add, v3, v2)
                v6 = tt(vv, prod[:, 0, :], vv, ALU.subtract, v4)
                last["prod"] = v6
                uf_tok[f, ch] = v6
                yield

    bg.append(spectrum())
    kn_tok, v2_tok, qn_tok, qp_tok = {}, {}, {}, {}
    for h in range(8):
        b = gemm(XB, [4, 5], c_ready)
        kn_tok[h] = evac(b, KN[:, h, :], xa_pe)
        if h % 2:
            background()
    drain_background()
    for h in range(8):
        b = gemm(XB, [4, 5], None)
        s = TT.next()
        v = evac(b, s.ap, *s.free)
        bt = MB.next()
        for tb in range(2):
            m = turn(bt.ap[:, tb * P:(tb + 1) * P], s.ap[:, tb * P:(tb + 1) * P], v, *bt.free)
        s.free = [m]
        v2_tok[h] = act(vt2[:, :, h * P:(h + 1) * P], bt.ap[:, 0:S].rearrange("p (b n) -> p b n", b=2), ACT.Copy,
                        m, last["utok"])
        bt.free = [v2_tok[h]]

    yh_tok = [None] * 8
    sY = Sum(SA[:, :], sQ.done)

    def inverse():
        for j in range(8):
            b = MB.next()
            n = 0
            for a_ in range(2):
                for f in range(2):
                    m = mm(b.ap[:, 0:S], UF[:, a_, f, j * P:(j + 1) * P], idft_b[:, a_, f, :], n == 0, n == 3,
                           uf_tok[f, j // 4], idft_tok, *b.free)
                    n += 1
            v = stt(UT[:, j, :], UT[:, j, :], pv("hyena_bias_2", j), b.ap[:, 0:S], ALU.mult, ALU.add, m)
            b.free = [v]
            yh_tok[j] = tt(UT[:, j, :], UT[:, j, :], X0[:, j, :], ALU.mult, v, x0_tok[j])
            sY.add(UT[:, j, :], yh_tok[j])
            last["uf"] = m
            yield

    PB2 = Turns([G2[:, 512 * i:512 * (i + 1)] for i in range(2)])
    PT2 = Turns([G2[:, 1024 + 512 * i:1536 + 512 * i] for i in range(2)])
    for s in PB2.slots + PT2.slots:
        s.free = [last["prod"]]
    ST2 = Turns([G3[:, 4096 + 8 * i:4104 + 8 * i] for i in range(3)])
    SC2 = float(192) ** -0.5
    oa_tok = [None] * 8
    sO = Sum(G2[:, 2048:2304], last["prod"])

    def head2(h):
        b = MB.next()
        for qb in range(2):
            q = slice(qb * P, (qb + 1) * P)
            mm(b.ap[:, qb * S:(qb + 1) * S], QN[:, h, q], KN[:, h, :], True, False, qn_tok[h], kn_tok[h], *b.free)
            m = mm(b.ap[:, qb * S:(qb + 1) * S], QP[:, h // 2, q], kpz[:, h % 2, :], False, True,
                   qp_tok[h // 2], kp_tok)
        pb, st = PB2.next(), ST2.next()
        p, x = pb.ap, st.ap
        v = vmax(x[:, 0:2], b.ap.rearrange("p (b n) -> p b n", b=2), m, *st.free)
        v = ts(x[:, 0:2], x[:, 0:2], -SC2, None, ALU.mult, None, v)
        for qb in range(2):
            a = act(p[:, qb * S:(qb + 1) * S], b.ap[:, qb * S:(qb + 1) * S], ACT.Exp, v, *pb.free,
                    bias=x[:, qb:qb + 1], scale=SC2, accum_out=x[:, 2 + qb:3 + qb])
        b.free = [a]
        v = recip(x[:, 2:4], x[:, 2:4], a)
        for qb in range(2):
            v1 = ts(p[:, qb * S:(qb + 1) * S], p[:, qb * S:(qb + 1) * S], x[:, 2 + qb:3 + qb], None, ALU.mult, None, v)
        st.free = [v1]
        yield
        b = MB.next()
        for kb in range(2):
            for qb in range(2):
                m = turn(b.ap[:, kb * S + qb * P:kb * S + qb * P + P], p[:, qb * S + kb * P:qb * S + kb * P + P],
                         v1, *b.free)
        pb.free = [m]
        pt = PT2.next()
        a = act(pt.ap, b.ap, ACT.Copy, m, *pt.free)
        b.free = [a]
        yield
        b = MB.next()
        for kb in range(2):
            m = mm(b.ap[:, 0:S], vt2[:, kb, h * P:(h + 1) * P], pt.ap[:, kb * S:(kb + 1) * S], kb == 0, kb == 1,
                   a, v2_tok[h], *b.free)
        pt.free = [m]
        oa_tok[h] = act(QN[:, h, :], b.ap[:, 0:S], ACT.Copy, m)
        b.free = [oa_tok[h]]
        sO.add(QN[:, h, :], oa_tok[h])
        yield

    bg.append(inverse())
    for h in range(8):
        b = gemm(XB, [0, 1, 2, 3], c_ready)
        qn_tok[h] = evac(b, QN[:, h, :], xa_pe)
        background()
    for t in range(4):
        b = gemm(XB, [0, 1, 2, 3], None)
        s = TT.next()
        v = evac(b, s.ap, *s.free)
        v = tt(QP[:, t, :], s.ap, rope[:, 0, :], ALU.mult, v, c_ready[-1])
        b = gemm(XB, [0, 1, 2, 3], None)
        v2 = evac(b, s.ap, v)
        v2 = tt(s.ap, s.ap, rope[:, 1, :], ALU.mult, v2)
        qp_tok[t] = tt(QP[:, t, :], QP[:, t, :], s.ap, ALU.add, v2, v)
        s.free = [qp_tok[t]]
        bg.append(head2(2 * t))
        bg.append(head2(2 * t + 1))
        background()
    c_pe = pe_last[0]
    drain_background()

    mx_ready = [None] * KT
    invy = sY.inv(INV[:, :], 1024, c_ready[3])
    mx_ready[0:8] = scaled(XA, lambda k: UT[:, k, :], yh_tok, INV[:, :], invy, lambda k: pv("hyena_out_gain_2", k),
                           last["uf"], n=8)
    io = G2[:, 2304:2560]
    invo = sO.inv(io, 1024)
    mx_ready[8:16] = scaled(XB, lambda k: QN[:, k, :], oa_tok, io, invo, lambda k: pv("attn_out_gain_2", k),
                            last["uf"], c_pe, n=8, at_=8)
    MX = G1
    mx_tok = [None] * KT
    mx_last = mx_ready[15]
    sM = Sum(SA[:, :], sY.done)
    for o in range(16):
        b = gemm(XA[0:8] + XB[8:16], ALLK, mx_ready)
        mx_tok[o] = evac(b, MX[:, o, :], mx_last)
        sM.add(MX[:, o, :], mx_tok[o])
    mx_pe = pe_last[0]
    invm = sM.inv(INV[:, :], DM, mx_ready[7])
    sH = Sum(SA[:, :], sM.done)
    for kt in range(KT):
        s = TT.next()
        v = stt(s.ap, MX[:, kt, :], pv("post_mix_gain_2", kt), INV[:, :], ALU.mult, ALU.mult, invm, mx_tok[kt], *s.free)
        res_tok[kt] = tt(RES[:, kt, :], RES[:, kt, :], s.ap, ALU.add, v, res_tok[kt])
        s.free = [res_tok[kt]]
        sH.add(RES[:, kt, :], res_tok[kt])
    invh = sH.inv(INV[:, :], DM, res_tok[15])
    hn_ready = scaled(XA, lambda k: RES[:, k, :], res_tok, INV[:, :], invh, lambda k: pv("pre_ffn_gain_2", k), mx_pe)

    FA = G2[:, :].rearrange("p (k n) -> p k n", k=KT)
    fa_tok = [mx_ready[15]] * KT
    f_last = [mx_pe]
    conv_in, conv_out = conv_buffers(G3[:, 0:1304], mx_ready[15], mx_pe)
    sE = Sum(SA[:, :], sH.done)
    for ci, ch in enumerate(CHUNKS):
        f_ready = [None] * KT
        for j, hh in enumerate(ch):
            b = gemm(XA, ALLK, hn_ready)
            s = conv_out.next()
            v = conv3(b, conv_in, s.ap, "ffn_conv_w_2", "ffn_conv_b_2", hh, NHID, *s.free)
            a = act(s.ap, s.ap, ACT.Gelu_apprx_tanh, v)
            b = gemm(XA, ALLK, None)
            s2 = EV.next()
            v = evac(b, s2.ap, *s2.free)
            v = tt(s.ap, s.ap, s2.ap, ALU.mult, v, a)
            s2.free = [v]
            _, v = put_split(XB, j, s.ap, v, f_last[0])
            s.free = [v]
            f_ready[j] = v
        for o in range(16):
            b = gemm(XB, list(range(len(ch))), f_ready)
            if ci == 0:
                fa_tok[o] = evac(b, FA[:, o, :], fa_tok[o])
            else:
                s = TT.next()
                v = evac(b, s.ap, *s.free)
                fa_tok[o] = tt(FA[:, o, :], FA[:, o, :], s.ap, ALU.add, v, fa_tok[o])
                s.free = [fa_tok[o]]
            if ci == len(CHUNKS) - 1:
                sE.add(FA[:, o, :], fa_tok[o])
        f_last[0] = pe_last[0]

    inve = sE.inv(INV[:, :], DM, hn_ready[15])
    OUT = G1[:, :, :].rearrange("p a n -> p (a n)").rearrange("p (b n) -> p b n", b=2)
    for g in range(4):
        bs = [MB.next(), MB.next()]
        for i in range(4):
            kt = 4 * g + i
            v = stt(FA[:, kt, :], FA[:, kt, :], pv("post_ffn_gain_2", kt), INV[:, :], ALU.mult, ALU.mult, inve, fa_tok[kt])
            v = tt(RES[:, kt, :], RES[:, kt, :], FA[:, kt, :], ALU.add, v, res_tok[kt])
            for tb in range(2):
                m = turn(bs[tb].ap[:, i * P:(i + 1) * P], RES[:, kt, tb * P:(tb + 1) * P], v, *bs[tb].free)
        for tb in range(2):
            a = act(OUT[:, tb, g * 512:(g + 1) * 512], bs[tb].ap, ACT.Copy, m, res_tok[15])
            bs[tb].free = [a]
        store(out[:, :, g * 512:(g + 1) * 512], OUT[:, :, g * 512:(g + 1) * 512], a)
    assert at["ring"] == len(plan) and at["sub"] == SUB and at["unit"] + 1 == at["split"], at
    Q.wait("sp", *stores)

    Q.count()
    block = ctx.enter_context(nc.Block())
    block.sync(lambda e: Q.emit("sp", e))
    block.scalar(lambda e: Q.emit("act", e))
    block.vector(lambda e: Q.emit("dve", e))
    block.tensor(lambda e: Q.emit("pe", e))


def tiled(w):
    k, n = w.shape
    return np.ascontiguousarray(w.reshape(k // P, P, n // P, P).transpose(2, 1, 0, 3)).reshape(n // P, P, k)


def tiled_parts(w):
    k, n = w.shape
    blocks = w.reshape(k // P, P, n // P, P).transpose(2, 0, 1, 3)
    tiles = []
    for c in CHUNKS:
        part = blocks[:, c.start:c.stop].reshape(-1, 16, P, P)
        tiles.append(part.transpose(0, 2, 1, 3).reshape(-1, P, 2048))
    return np.ascontiguousarray(np.concatenate(tiles))


def packed(blocks):
    return np.ascontiguousarray(np.stack(blocks).reshape(-1, 16, P, P).transpose(0, 2, 1, 3)).reshape(-1, P, 2048)


def blocks_of(w):
    return [w[i:i + P] for i in range(0, w.shape[0], P)]


def constants():
    f64 = np.float64
    n = 2 * S - 1
    t = np.arange(S, dtype=f64)
    f = np.arange(S, dtype=f64)
    ang = 2 * np.pi * ((t[:, None] * f[None, :]) % n) / n
    dft = np.stack([np.cos(ang), np.sin(ang)]).reshape(2, 2, P, S).transpose(2, 0, 1, 3)
    wf = np.where(f == 0, 1.0, 2.0)[:, None] / n
    idft = np.stack([wf * np.cos(ang.T), -wf * np.sin(ang.T)]).reshape(2, 2, P, S).transpose(2, 0, 1, 3)
    f32 = np.float32
    lin = np.linspace(0.0, 1.0, S).astype(f32)
    w = (2.0 * np.pi * np.arange(S) / S).astype(f32)
    fr = np.linspace(1e-4, 15, 16).astype(f32)
    a = (w[:, None] * fr[None, :]).astype(f32).astype(f64)
    z = np.concatenate([lin[:, None].astype(f64), np.cos(a), -np.sin(a)], axis=1)
    lo, hi = np.log(1e-2) / 1.5, np.log(1e-2) / 0.3
    deltas = np.abs(np.linspace(lo, hi, 1024)).astype(f32)
    win = np.exp(-(lin[:, None] * deltas[None, :]).astype(f64)) + 0.05
    back = win.copy()
    back[0] = 0.0
    window = np.stack([win, back]).reshape(2, 2, P, 1024).transpose(2, 0, 1, 3)
    inv = (1.0 / (f32(10000.0) ** (np.arange(0, 64, 2, dtype=f32) / f32(64)))).astype(f32)
    ra = (np.arange(S, dtype=f32)[:, None] * inv[None, :]).astype(f32).astype(f64)
    cos, sin = np.cos(ra).T, np.sin(ra).T
    rope = np.stack([np.concatenate([cos] * 4), np.concatenate([-sin, sin] * 2)]).transpose(1, 0, 2)
    q, k = np.arange(P)[:, None], np.arange(S)[None, :]
    mask = np.where((k > q) & (k <= q + P), 0.0, -1e30)
    out = {"dft": dft, "idft": idft, "zT": z.T, "window": window, "rope": rope, "mask": mask, "ident": np.eye(P)}
    return {k: np.ascontiguousarray(v.astype(f32)) for k, v in out.items()}


def layout(x):
    a = constants()
    cols = {}
    for name in PV:
        if name in ("sinks", "filt"):
            continue
        v = np.asarray(x[name], dtype=x[name].dtype)
        cols[name] = v.reshape(-1, P).T
    cols["sinks"] = np.broadcast_to(x["sinks"].reshape(1, 16), (P, 16))
    filt = [x[k].reshape(64) for k in ("filt_freq1_2", "filt_b1_2", "filt_freq2_2", "filt_b2_2")]
    pad = np.zeros(64, np.float32)
    cols["filt"] = np.stack([np.concatenate([v, pad]) for v in filt], axis=1)
    a["pv"] = np.ascontiguousarray(np.concatenate([cols[k] for k in PV], axis=1))
    a["x"] = np.ascontiguousarray(x["x"].reshape(2, P, DM).transpose(1, 0, 2))
    a["ada"] = np.ascontiguousarray(x["ada_w"].reshape(8, 2, P, 12, 1024).transpose(3, 0, 2, 1, 4)).reshape(12, 8, P, 2048)
    lw = np.stack([x["lru_wa"].reshape(16, P, P), x["lru_wx"].reshape(16, P, P)])
    a["lru_w"] = np.ascontiguousarray(lw.transpose(2, 0, 1, 3))
    for name in ("w_in", "w_lru_out", "w_attn_out", "w_o", "w_ffn_in"):
        a[name] = tiled(x[name][0])
    a["w_ffn_out"] = tiled_parts(x["w_ffn_out"][0])
    w = x["w_in_2"][0]
    pe = w[:, 3840:3904]
    rot = np.concatenate([pe[:, 32:], pe[:, :32]], axis=1)
    a["w_in2"] = tiled(np.concatenate([w[:, :3840], pe, pe, rot, rot], axis=1))
    ukv = x["w_ukv_2"][0].reshape(256, 8, 2, P)
    uq = x["w_uq_2"][0].reshape(512, 8, 192)
    blocks = []
    for part in range(2):
        for h in range(8):
            blocks += blocks_of(ukv[:, h, part])
    for h in range(8):
        blocks += blocks_of(uq[:, h, :P])
    for t in range(4):
        pes = [uq[:, 2 * t + i, P:] for i in range(2)]
        blocks += blocks_of(np.concatenate(pes, axis=1))
        blocks += blocks_of(np.concatenate([y for q in pes for y in (q[:, 32:], q[:, :32])], axis=1))
    a["w_u2"] = packed(blocks)
    a["w_out2"] = tiled(x["w_out_2"][0])
    a["w_up2"] = tiled(x["w_up_2"][0])
    a["w_down2"] = tiled_parts(x["w_down_2"][0])
    for name in ("filt_w1_2", "filt_w2_2", "filt_w3_2"):
        a[name] = np.ascontiguousarray(x[name][0])
    return a


def kernel(**inputs):
    import concourse.bacc as bacc
    from concourse.bass_utils import run_bass_kernel_spmd

    arrays = {f"in_{k}": v for k, v in layout({k: np.asarray(v) for k, v in inputs.items()}).items()}
    nc = bacc.Bacc("TRN2", target_bir_lowering=False, num_devices=1)
    d = {}
    for name, a in arrays.items():
        d[name[3:]] = nc.dram_tensor(name, a.shape, mybir.dt.from_np(a.dtype), kind="ExternalInput").ap()
    out = nc.dram_tensor("out", (1, S, DM), F32, kind="ExternalOutput").ap()
    program(nc, d, out.rearrange("a (b p) n -> p (a b) n", p=P))
    r = run_bass_kernel_spmd(nc, [arrays], core_ids=[0])
    return r.results[0]["out"]
```

```python
from contextlib import ExitStack

import numpy as np

import concourse.bass as bass
import concourse.mybir as mybir

F32 = mybir.dt.float32
F32R = mybir.dt.float32r
ALU = mybir.AluOpType
ACT = mybir.ActivationFunctionType
AX = mybir.AxisListType
P = 128
S = 256
DM = 2048
KT = 16
NHID = 44
CHUNKS = [range(0, 15), range(15, 30), range(30, 44)]
EPS = 1e-6
RING = 6
USLOTS = 4
SUB = 8
LOWS = 5
ADA_PE = (1, 3, 6, 8, 10, 13, 15)

PV = {}
_n = 0
for _name, _w in [("norm1_g", 16), ("b_in", 88), ("conv_w", 64), ("conv_b", 16), ("lru_ba", 16), ("lru_bx", 16),
                  ("lru_lambda", 16), ("norm2_g", 16), ("final_g", 16), ("c", 16), ("ada_b", 96), ("sinks", 16),
                  ("pre_mix_gain_2", 16), ("hyena_conv_w_2", 72), ("hyena_conv_b_2", 24), ("hyena_bias_2", 8),
                  ("q_norm_gain_2", 4), ("kv_norm_gain_2", 2), ("hyena_out_gain_2", 8), ("attn_out_gain_2", 8),
                  ("post_mix_gain_2", 16), ("pre_ffn_gain_2", 16), ("ffn_conv_w_2", 132), ("ffn_conv_b_2", 44),
                  ("post_ffn_gain_2", 16), ("filt", 4)]:
    PV[_name] = _n
    _n += _w
NPV = _n


class Tok:

    def __init__(self, eng, sem=None, value=None):
        self.eng, self.sem, self.value, self.used = eng, sem, value, False


class Queues:

    def __init__(self, sems):
        self.q = {k: [] for k in sems}
        self.sems = sems

    def op(self, eng, fn, *waits):
        self.wait(eng, *waits)
        t = Tok(eng)
        self.q[eng].append((t, fn))
        return t

    def wait(self, eng, *toks):
        for t in toks:
            if t is None:
                continue
            if isinstance(t, (list, tuple)):
                self.wait(eng, *t)
                continue
            t.used = True
            self.q[eng].append((t, None))

    def count(self):
        for eng, items in self.q.items():
            n = 0
            for t, fn in items:
                if fn is not None and t.used and t.sem is None:
                    n += 1
                    t.sem, t.value = self.sems[eng], n

    def emit(self, eng, e):
        seen = {}
        for t, fn in self.q[eng]:
            if fn is None:
                if seen.get(id(t.sem), 0) < t.value:
                    e.wait_ge(t.sem, t.value)
                    seen[id(t.sem)] = t.value
            else:
                ins = fn(e)
                if t.used and t.eng != "dma":
                    ins.then_inc(t.sem, 1)


class Slot:

    def __init__(self, ap):
        self.ap, self.held, self._free = ap, False, []

    @property
    def free(self):
        return self._free

    @free.setter
    def free(self, toks):
        self._free, self.held = toks, False


class Turns:
    def __init__(self, aps):
        self.slots, self.n = [Slot(a) for a in aps], 0

    def next(self):
        s = self.slots[self.n % len(self.slots)]
        assert not s.held
        s.held = True
        self.n += 1
        return s


RAMPS = {"w_in": (0, 1, 2, 3), "w_ffn_in": (0, NHID, 1, NHID + 1), "w_in2": (24, 25, 26, 27), "w_out2": (0, 1, 2, 3),
         "w_up2": (0, NHID, 1, NHID + 1)}


def halves(tiles):
    return [(*tile, half) for tile in tiles for half in range(2)]


def ring_plan():
    plan = [("ada", s, j) for s in (2, 3, 0, 1) for j in range(8)]
    plan[-3:-3] = [("w_in", 0), ("w_in", 1)]
    plan = halves(plan)
    w = [("w_in", o) for o in range(2, 16)]
    w += [("w_in", 48 + o) for o in range(8)]
    w += [("w_in", 32 + o) for o in range(16)]
    w += [("w_in", 16 + o) for o in range(16)]
    for o in range(16):
        w += [("w_in", 56 + o), ("w_lru_out", o)]
    w += [("w_in", 72 + o) for o in range(16)]
    w += [("w_attn_out", o) for o in range(16)]
    w += [("w_o", o) for o in range(16)]
    base = 0
    for c in CHUNKS:
        for h in c:
            w += [("w_ffn_in", h), ("w_ffn_in", NHID + h)]
        w += [("w_ffn_out", base + j) for j in range(len(c))]
        base += len(c)
    ada = halves([("ada", s, j) for s in range(4, 12) for j in range(8)])
    for n, item in enumerate(halves(w), 4):
        plan.append(item)
        while ada and n >= 20 + 2.4 * (128 - len(ada)):
            plan.append(ada.pop(0))
    assert not ada
    first, plan = plan, []
    plan += [("w_in2", 24 + j) for j in range(8)]
    for j in range(8):
        plan += [("w_in2", 8 + j), ("w_in2", 16 + j)]
        if j == 1:
            plan += [("w_u2", i) for i in range(6)]
    plan += [("w_in2", j) for j in range(8)]
    plan += [("w_out2", o) for o in range(16)]
    base = 0
    for c in CHUNKS:
        for h in c:
            plan += [("w_up2", h), ("w_up2", NHID + h)]
        plan += [("w_down2", base + j) for j in range(len(c))]
        base += len(c)
    return first + halves(plan)


def program(nc, d, out):
    ctx = ExitStack()
    with ctx:
        _program(nc, d, out, ctx)


def _program(nc, d, out, ctx):
    def sb(name, shape, dt=F32):
        return ctx.enter_context(nc.sbuf_tensor(name, shape, dt))

    def overlay(*views):
        made = []
        for name, shape, dt in views[:-1]:
            with nc.sbuf_tensor(name, shape, dt) as t:
                made.append(t)
        return made + [sb(*views[-1])]

    sems = {k: ctx.enter_context(nc.semaphore("s_" + k)) for k in ("pe", "act", "dve", "pool", "sp")}
    Q = Queues(sems)
    dsem = [ctx.enter_context(nc.semaphore(f"s_ring{i}")) for i in range(RING)]

    W = sb("W", [P, RING, 1024])
    WH = sb("WH", [P, USLOTS, SUB * P], F32R)
    WL = sb("WL", [P, USLOTS, SUB * P], F32R)
    XA_, XAf = overlay(("XA", [P, KT, 512], F32R), ("XAf", [P, 8192], F32))
    XA = [XA_[:, k, :] for k in range(KT)]
    XB_, XBf = overlay(("XB", [P, KT, 512], F32R), ("XBf", [P, 8192], F32))
    XB = [XB_[:, k, :] for k in range(KT)]
    RES = sb("RES", [P, KT, S])
    G1 = sb("G1", [P, KT, S])
    G2 = sb("G2", [P, 4096])
    G3 = sb("G3", [P, 4160])
    ACC = sb("ACC", [P, 2, 1024])
    PVT = sb("PVT", [P, NPV])
    IDN = sb("IDN", [P, P])
    ONE = sb("ONE", [P, P])
    MOD = sb("MOD", [P, 96])
    SM = sb("SM", [P, 128])
    SA = sb("SA", [P, S])
    INV = sb("INV", [P, S])
    EV = Turns([sb(f"EV{i}", [P, S])[:, :] for i in range(4)])
    TT = Turns([sb(f"TT{i}", [P, S])[:, :] for i in range(3)])
    PS = [ctx.enter_context(nc.psum_tensor(f"PS{i}", [P, 512], F32)) for i in range(8)]
    GB = Turns([PS[i][:, :] for i in range(4)])
    MB = Turns([PS[i][:, :] for i in range(4, 8)])

    def pv(name, j=0, n=1):
        return PVT[:, PV[name] + j:PV[name] + j + n]

    def tt(o, a, b, op, *w):
        return Q.op("dve", lambda e: e.tensor_tensor(o, a, b, op), *w)

    def stt(o, a, s, b, op0, op1, *w):
        return Q.op("dve", lambda e: e.scalar_tensor_tensor(out=o, in0=a, scalar=s, in1=b, op0=op0, op1=op1), *w)

    def ts(o, a, s1, s2, op0, op1, *w):
        if s2 is None:
            return Q.op("dve", lambda e: e.tensor_scalar(o, a, s1, None, op0), *w)
        return Q.op("dve", lambda e: e.tensor_scalar(o, a, s1, s2, op0, op1), *w)

    def vcopy(o, a, *w):
        return Q.op("dve", lambda e: e.tensor_copy(o, a), *w)

    def recip(o, a, *w):
        return Q.op("dve", lambda e: e.reciprocal(o, a), *w)

    def vmax(o, a, *w):
        return Q.op("dve", lambda e: e.tensor_reduce(o, a, AX.X, ALU.max), *w)

    def memset(o, v, *w):
        return Q.op("dve", lambda e: e.memset(o, v), *w)

    def act(o, a, f, *w, **kw):
        return Q.op("act", lambda e: e.activation(o, a, f, **kw), *w)

    def mm(o, l, r, start, stop, *w):
        return Q.op("pe", lambda e: e.matmul(o, l, r, start=start, stop=stop, skip_group_check=True), *w)

    def turn(o, a, *w):
        return Q.op("pe", lambda e: e.transpose(o, a, IDN[:, :]), *w)

    nload = [0]

    def load(o, a, *w):
        eng = "pool" if w else "sp"
        s = ctx.enter_context(nc.semaphore(f"s_load{nload[0]}"))
        nload[0] += 1
        t = Tok("dma", s, 16)
        Q.wait(eng, *w)
        Q.q[eng].append((t, lambda e: e.dma_start(o, a).then_inc(s, 16)))
        return t

    plan = ring_plan()
    ring_free = [[] for _ in plan]
    ring_tok = []

    def ring_load():
        n = len(ring_tok)
        if n == len(plan):
            return
        if n >= RING:
            Q.wait("sp", *ring_free[n - RING])
        kind = plan[n]
        src = (d["ada"][kind[1], kind[2]] if kind[0] == "ada" else d[kind[0]][kind[1]])[:, kind[-1] * 1024:(kind[-1] + 1) * 1024]
        s, v, slot = dsem[n % RING], 16 * (n // RING + 1), n % RING
        t = Tok("dma", s, v)
        Q.q["sp"].append((t, lambda e: e.dma_start(W[:, slot, :], src).then_inc(s, 16)))
        ring_tok.append(t)

    at = {"ring": 0, "split": 0, "unit": -1, "sub": SUB}
    unit_tok = []
    unit_done = []
    ada_free = [[], []]
    mod_tok = {}
    c_tok = []

    def ada_tile(n):
        _, s, j, half = plan[n]
        acc, src, k = ACC[:, s % 2, :], W[:, n % RING, :], 2 * j + half
        c = SM[:, k:k + 1]
        if s < 4 and k in ADA_PE:
            banks = GB.slots[2 * (s % 2):2 * (s % 2) + 2]
            for i, b in enumerate(banks):
                t = mm(b.ap[0:1, :], c, src[:, i * 512:(i + 1) * 512], k == ADA_PE[0], k == 15, ring_tok[n],
                       *c_tok, *(b.free if k == ADA_PE[0] else []))
            ring_free[n] = [t]
            if k == 15:
                for i, b in enumerate(banks):
                    part = acc[0:1, i * 512:(i + 1) * 512]
                    v = tt(part, part, b.ap[0:1, :], ALU.add, t, ada_last[0])
                    b.free = [v]
                ada_pending.append((s, v, at["unit"]))
            return
        if k == 0:
            while any(p[0] % 2 == s % 2 for p in ada_pending):
                ada_reduce()
            t = ts(acc, src, c, None, ALU.mult, None, ring_tok[n], *c_tok, *ada_free[s % 2])
        else:
            t = stt(acc, src, c, acc, ALU.mult, ALU.add, ring_tok[n], ada_last[0])
        ada_last[0] = t
        ring_free[n] = [t]
        if k == 15:
            ada_pending.append((s, t, at["unit"]))

    ada_last = [None]
    ada_pending = []

    def ada_reduce(age=0):
        while ada_pending and at["unit"] >= ada_pending[0][2] + age:
            s, t, _ = ada_pending.pop(0)
            b = MB.next()
            for i in range(8):
                m = mm(b.ap[:, i:i + 1], ACC[:, s % 2, i * P:(i + 1) * P], ONE[:, 0:1], True, True,
                       t, ones_tok[0], *b.free)
            ada_free[s % 2] = [m]
            mod_tok[s] = tt(MOD[:, 8 * s:8 * s + 8], b.ap[:, 0:8], pv("ada_b", 8 * s, 8), ALU.add, m, pv_tok[0])
            b.free = [mod_tok[s]]

    def split_next():
        while at["ring"] < len(plan) and plan[at["ring"]][0] == "ada":
            split_lows()
            ada_tile(at["ring"])
            at["ring"] += 1
            ring_load()
        if at["ring"] == len(plan):
            return
        n, u = at["ring"], at["split"]
        src = W[:, n % RING, :]
        hi, lo = WH[:, u % USLOTS, :], WL[:, u % USLOTS, :]
        before = [unit_done[u - USLOTS]] if u >= USLOTS else []
        a = act(hi, src, ACT.Copy, ring_tok[n], *before)
        at["split"] += 1
        at["ring"] += 1

        def low():
            v = tt(lo, src, hi.bitcast(F32), ALU.subtract, a, *before)
            unit_tok.append(v)
            ring_free[n] = [v]
            ring_load()
        lows.append(low)

    lows = []

    def split_lows():
        while lows:
            lows.pop(0)()

    def next_sub():
        if at["sub"] == SUB:
            background()
            ada_reduce(4)
            at["unit"] += 1
            at["sub"] = 0
            while at["split"] < at["unit"] + USLOTS and at["ring"] < len(plan):
                split_next()
            soon_step()
            if len(unit_tok) <= at["unit"]:
                split_lows()
            Q.wait("pe", unit_tok[at["unit"]])
        i = at["sub"]
        at["sub"] += 1
        if i == LOWS:
            split_lows()
            if width[0] > 2:
                background()
        return at["unit"] % USLOTS, i

    def gemm(X, kts, ready):
        if ramped:
            return ramped.pop(0)
        b = GB.next()
        n = len(kts)
        for j, kt in enumerate(kts):
            u, i = next_sub()
            while ready and ready[kt] is None:
                soon_step()
            hi, lo = WH[:, u, i * P:(i + 1) * P], WL[:, u, i * P:(i + 1) * P]
            mm(b.ap, hi, X[kt], j == 0, False, *(b.free if j == 0 else []), ready[kt] if ready else None)
            m = mm(b.ap[:, S:2 * S], lo, X[kt][:, 0:S], False, j == n - 1)
            if at["sub"] == SUB:
                unit_done.append(m)
        b.done = m
        pe_last[0] = m
        return b

    ramped = []

    def ramp(X, kts, make):
        bs = [GB.next() for _ in range(4)]
        ready, n, begun = [], len(kts), []
        for j, kt in enumerate(kts):
            while len(ready) < min(j + 4, n):
                if len(begun) < n:
                    begun.append(make(kts[len(begun)]))
                if len(begun) > len(ready) + 1 or len(begun) == n:
                    ready.append(begun[len(ready)]())
            for b in bs:
                u, i = next_sub()
                hi, lo = WH[:, u, i * P:(i + 1) * P], WL[:, u, i * P:(i + 1) * P]
                mm(b.ap, hi, X[kt], j == 0, False, *(b.free if j == 0 else []), ready[j])
                b.done = mm(b.ap[:, S:2 * S], lo, X[kt][:, 0:S], False, j == n - 1)
                if at["sub"] == SUB:
                    unit_done.append(b.done)
        pe_last[0] = bs[-1].done
        ramped.extend(bs)
        return ready[-1]

    pe_last = [None]
    first, second = [], []
    steps = [0]
    SPACE = {2: 2, 3: 3}

    def later(g):
        second.append([g, steps[0]])

    def background():
        steps[0] += 1
        if first:
            if next(first[0], "end") == "end":
                first.pop(0)
            return
        for e in second[:width[0]]:
            if steps[0] - e[1] >= SPACE[width[0]]:
                e[1] = steps[0]
                if next(e[0], "end") == "end":
                    second.remove(e)
                return

    width = [2]

    def drain_background():
        while first or second:
            background()

    def evac(b, o, *w, bias=None, scale=None):
        t = EV.next()
        kw = {}
        if bias is not None:
            kw["bias"] = bias
        if scale is not None:
            kw["scale"] = scale
        a = act(t.ap, b.ap[:, S:2 * S], ACT.Identity, b.done, *t.free, **kw)
        if scale is None:
            v = tt(o, b.ap[:, 0:S], t.ap, ALU.add, a, *w)
        else:
            v = stt(o, b.ap[:, 0:S], scale, t.ap, ALU.mult, ALU.add, a, *w)
        b.free = [v]
        t.free = [v]
        return v

    soon = []

    def soon_step():
        soon[:] = [g for g in soon if next(g, "end") != "end"]

    def split_later(X, kt, src, s, ready, tok, *w):
        def run():
            a = act(X[kt][:, 0:S], src, ACT.Copy, tok, *w)
            yield
            ready[kt] = tt(X[kt][:, S:2 * S], src, X[kt][:, 0:S].bitcast(F32), ALU.subtract, a)
            if s is not None:
                s.free = [ready[kt]]
        soon.append(run())

    def soon_all():
        while soon:
            soon_step()

    def root_table():
        act(SM[:, 113:114], SM[:, 112:113], ACT.Sqrt)

    class Sum:

        def __init__(self, acc, *w):
            self.acc, self.last, self.w = acc, None, list(w)

        def add(self, src, *w, scale=None):
            kw = {} if scale is None else {"scale": scale}
            if self.last is None:
                self.last = act(self.acc, src, ACT.Square, *w, *self.w, **kw)
                return self.last
            t = TT.next()
            a = act(t.ap, src, ACT.Square, *w, *t.free, **kw)
            self.last = tt(self.acc, self.acc, t.ap, ALU.add, a, self.last)
            t.free = [self.last]
            return a

        def add_later(self, src, tok, scale=None):
            def run():
                kw = {} if scale is None else {"scale": scale}
                t = TT.next()
                a = act(t.ap, src, ACT.Square, tok, *t.free, **kw)
                yield
                self.last = tt(self.acc, self.acc, t.ap, ALU.add, a, self.last)
                t.free = [self.last]
            if self.last is None:
                self.add(src, tok, scale=scale)
            else:
                soon.append(run())

        def inv(self, o, n, *w):
            b = MB.next()
            m = mm(b.ap[:, 0:S], ONE[:, :], self.acc, True, True, self.last, ones_tok[0], *b.free)
            self.done = m
            a = act(o, b.ap[:, 0:S], ACT.Sqrt, m, *w, scale=1.0 / n, bias=SM[:, 112:113])
            b.free = [a]
            return recip(o, o, a)

    pv_tok = [load(PVT[:, :], d["pv"])]
    for _ in range(RING):
        ring_load()
    x_view = XAf[:, 0:4096].rearrange("p (b n) -> p b n", b=2)
    w3 = XBf[0:64, 4096:6144]
    zT = XBf[0:33, 6144:6400]
    w1 = XBf[0:33, 6400:6464]
    w2 = XBf[0:64, 6464:6528]
    fs = XBf[0:64, 6528:7808].rearrange("p (a n) -> p a n", a=5)
    CS = G3[:, 0:1024].rearrange("p (a b f) -> p a b f", a=2, b=2)
    win = XAf[:, 4096:6144].rearrange("p (b n) -> p b n", b=2)
    lw = G2[:, :].rearrange("p (a h n) -> p a h n", a=2, h=16)
    z_tok = [load(zT, d["zT"]), load(w1, d["filt_w1_2"]), load(w2, d["filt_w2_2"])]

    ones_tok = [memset(ONE[:, :], 1.0)]
    eps_tok = memset(SM[:, 112:113], EPS)
    c_tok.append(act(SM[:, 0:16], pv("c", 0, 16), ACT.Silu, pv_tok[0]))

    res_tok = [None] * KT
    s1 = Sum(SA[:, :])
    norm1 = {}

    def x_turns():
        for j in range(8):
            b = MB.next()
            for i in range(2):
                for tb in range(2):
                    m = turn(b.ap[:, i * S + tb * P:i * S + tb * P + P],
                             x_view[:, tb, (2 * j + i) * P:(2 * j + i + 1) * P], x_tok, id_tok, *b.free)
            a = act(RES[:, 2 * j:2 * j + 2, :].rearrange("p a n -> p (a n)"), b.ap, ACT.Copy, m)
            b.free = [a]
            res_tok[2 * j] = res_tok[2 * j + 1] = a
            norm1["read"] = m
            yield
            for kt in (2 * j, 2 * j + 1):
                s1.add(RES[:, kt, :], res_tok[kt])
        norm1["inv"] = s1.inv(INV[:, :], DM, eps_tok)

    lam = pv("lru_lambda", 0, 16)
    lp = [SM[:, 16 * i:16 * i + 16] for i in range(1, 6)]
    a = act(lp[0], lam, ACT.Abs, pv_tok[0])
    a = act(lp[1], lp[0], ACT.Exp, a, scale=-1.0)
    v = ts(lp[2], lp[1], 2.0, None, ALU.add, None, a)
    v = recip(lp[2], lp[2], v)
    v = tt(lp[2], lp[1], lp[2], ALU.mult, v)
    v = tt(lp[3], lp[2], lp[2], ALU.mult, v)
    v = ts(lp[4], lp[3], 1.0 / 19, 1.0 / 17, ALU.mult, ALU.add, v)
    for k in (15, 13, 11, 9, 7, 5, 3, 1):
        v = tt(lp[4], lp[4], lp[3], ALU.mult, v)
        v = ts(lp[4], lp[4], 1.0 / k, None, ALU.add, None, v)
    v = tt(lp[4], lp[4], lp[2], ALU.mult, v)
    v1 = ts(lp[0], lam, -1.0, 0.0, ALU.mult, ALU.max, pv_tok[0], v)
    v = stt(lp[0], lp[4], 2.0, lp[0], ALU.mult, ALU.add, v1)
    SP = lp[2]
    SN = lp[3]
    v = ts(SP, lp[0], 8.0, None, ALU.mult, None, v)
    sp_tok = ts(SN, lp[0], -8.0, None, ALU.mult, None, v)

    kf_dram = nc.dram_tensor("kf", [P, 4096], F32, kind="Internal").ap()

    def sine(arg, o, t1, *w):
        mg = 12582912.0
        v = ts(t1, arg, 1.0 / (2 * np.pi), mg, ALU.mult, ALU.add, *w)
        v = ts(t1, t1, -mg, None, ALU.add, None, v)
        c1 = 6.28125
        c2 = round((2 * np.pi - c1) * 2.0**21) / 2.0**21
        c3 = float(2 * np.pi - c1 - c2)
        for c in (c1, c2, c3):
            v = stt(arg, t1, -c, arg, ALU.mult, ALU.add, v)
        v = ts(arg, arg, 3.1415925, -3.1415925, ALU.min, ALU.max, v)
        return act(o, arg, ACT.Sin, v)

    def filters():
        def layer(lhsT, rhs, k, *w):
            b = MB.next()
            m = mm(b.ap[0:64, 0:S], lhsT, rhs, True, True, *w, *b.free)
            freq, bias = (PVT[0:64, PV["filt"] + i:PV["filt"] + i + 1] for i in (k, k + 1))
            v = ts(fs[:, 0, :], b.ap[0:64, 0:S], bias, freq, ALU.add, ALU.mult, m, pv_tok[0])
            b.free = [v]
            return v

        v = layer(w1, zT, 0, *z_tok)
        yield
        a = sine(fs[:, 0, :], fs[:, 1, :], fs[:, 2, :], v)
        yield
        v = layer(w2, fs[:, 1, :], 2, a)
        yield
        a = sine(fs[:, 0, :], fs[:, 1, :], fs[:, 2, :], v)
        yield
        yield
        pq = XBf[:, 0:4096].rearrange("p (a b n) -> p a b n", a=2, b=2)
        tmp = G1[:, 0:4, :].rearrange("p (a b) n -> p a (b n)", a=2)
        toks = []
        v2 = None
        for tb in range(2):
            for ch in range(2):
                bf, bb = MB.next(), MB.next()
                mf = mm(bf.ap, fs[:, 1, tb * P:(tb + 1) * P], w3[:, ch * 512:(ch + 1) * 512], True, True, a, w3_tok, *bf.free)
                mb = mm(bb.ap, fs[:, 1, tb * P:(tb + 1) * P], w3[:, 1024 + ch * 512:1024 + (ch + 1) * 512], True, True, *bb.free)
                va = tt(tmp[:, 0, :], bf.ap, win[:, tb, ch * 512:(ch + 1) * 512], ALU.mult, mf, win_tok, v2)
                vb = tt(tmp[:, 1, :], bb.ap, win[:, tb, ch * 512:(ch + 1) * 512], ALU.mult, mb)
                if tb == 0:
                    vb = memset(tmp[0:1, 1, :], 0.0, vb)
                bf.free, bb.free = [va], [vb]
                tt(pq[:, 0, tb, ch * 512:(ch + 1) * 512], tmp[:, 0, :], tmp[:, 1, :], ALU.add, va, vb)
                v2 = tt(pq[:, 1, tb, ch * 512:(ch + 1) * 512], tmp[:, 1, :], tmp[:, 0, :], ALU.subtract)
                toks.append(v2)
                yield
        kf = G1[:, :, :].rearrange("p a n -> p (a n)").rearrange("p (a f n) -> p a f n", a=2, f=2)
        for a_ in range(2):
            for f in range(2):
                for ch in range(2):
                    b = MB.next()
                    for tb in range(2):
                        m = mm(b.ap, CS[:, a_, tb, f * P:(f + 1) * P], pq[:, a_, tb, ch * 512:(ch + 1) * 512],
                               tb == 0, tb == 1, toks[-1], cs_tok, *b.free)
                    c = act(kf[:, a_, f, ch * 512:(ch + 1) * 512], b.ap, ACT.Copy, m, toks[-1])
                    b.free = [c]
                    yield
        g1_free.append(c)
        xb_free.append(m)
        xa_free.append(toks[-1])
        g3_free.append(m)

    stores = []

    def store(o, a, *w):
        s = ctx.enter_context(nc.semaphore(f"s_store{len(stores)}"))
        t = Tok("dma", s, 16)
        Q.wait("pool", *w)
        Q.q["pool"].append((t, lambda e: e.dma_start(o, a).then_inc(s, 16)))
        stores.append(t)
        return t

    g1_free, xa_free, xb_free, g3_free = [], [], [], []

    flt, xt = filters(), x_turns()
    for n in range(68):
        if plan[n][0] == "ada":
            ada_tile(n)
            at["ring"] += 1
            ring_load()
        else:
            split_next()
            split_lows()
        if n % 16 == 2:
            ada_reduce()
        if n == 1:
            w3_tok = load(w3, d["filt_w3_2"], ring_tok[6])
            cs_tok = load(CS, d["dft"], ring_tok[6])
            win_tok = load(win, d["window"], ring_tok[6])
            id_tok = load(IDN[:, :], d["ident"], ring_tok[6])
        if n == 5:
            x_tok = load(x_view, d["x"], ring_tok[10])
        if n >= 16 and n % 4 == 0:
            next(xt, None)
        if n > 3 and n % 4 == 1:
            next(flt, None)
    for _ in flt:
        pass
    for _ in xt:
        pass
    g1_free[:] = [store(kf_dram, G1[:, :, :].rearrange("p a n -> p (a n)"), ring_tok[70], *g1_free)]
    lw_tok = load(lw, d["lru_w"], ring_tok[71])
    inv_tok, x_read = norm1["inv"], norm1["read"]

    SC = SM[:, 96:112]

    def scale_of(g, first):
        return stt(SC, MOD[:, first:first + 16], 1.0, pv(g, 0, 16), ALU.add, ALU.mult,
                   mod_tok[first // 8], mod_tok[first // 8 + 1])

    ada_reduce()
    sc_tok = scale_of("norm1_g", 16)

    def modulated(X, shift, sc, it, *w):
        def make(kt):
            t = TT.next()
            v = stt(t.ap, RES[:, kt, :], SC[:, kt:kt + 1], INV[:, :], ALU.mult, ALU.mult, sc, it, res_tok[kt], *t.free)
            sh = MOD[:, shift + kt:shift + kt + 1]
            a = act(X[kt][:, 0:S], t.ap, ACT.Identity, v, mod_tok[shift // 8], mod_tok[shift // 8 + 1], *w, bias=sh)

            def end():
                v = stt(X[kt][:, S:2 * S], t.ap, sh, X[kt][:, 0:S].bitcast(F32), ALU.add, ALU.subtract, a)
                t.free = [v]
                return v
            return end
        return make

    def scaled(X, kt, src, tok, inv, it, gain, *w):
        t = TT.next()
        v = stt(t.ap, src, gain, inv, ALU.mult, ALU.mult, it, tok, *t.free)
        a = act(X[kt][:, 0:S], t.ap, ACT.Copy, v, *w)

        def end():
            v = tt(X[kt][:, S:2 * S], t.ap, X[kt][:, 0:S].bitcast(F32), ALU.subtract, a)
            t.free = [v]
            return v
        return end

    ALLK = list(range(KT))
    h_last = ramp(XA, ALLK, modulated(XA, 0, sc_tok, inv_tok, x_read, *xa_free))

    Y = G1
    LS = XBf[:, 0:6144].rearrange("p (a n) -> p a n", a=6)
    UP = Turns([XBf[:, 6144 + 264 * i:6144 + 264 * i + 259] for i in range(2)])
    for s in UP.slots:
        s.free = [memset(s.ap[:, 0:3], 0.0, *xb_free)]
    uc_tok = [None] * 16
    y_tok = [None] * 16
    ls_free, ri_free = [], [[], []]

    def lru_batch(q):
        yield
        R4, I4, T4, A4 = LS[:, 2 * (q % 2), :], LS[:, 2 * (q % 2) + 1, :], LS[:, 4, :], LS[:, 5, :]
        for j in range(4):
            h = 4 * q + j
            b = MB.next()
            m = mm(b.ap[:, 0:S], lw[:, 0, h, :], Y[:, h, :], True, True, uc_tok[h], lw_tok, *b.free)
            m = mm(b.ap[:, S:2 * S], lw[:, 1, h, :], Y[:, h, :], True, True)
            a = act(R4[:, j * S:(j + 1) * S], b.ap[:, 0:S], ACT.Sigmoid, m, *ri_free[q % 2], *xb_free, bias=pv("lru_ba", h))
            a = act(I4[:, j * S:(j + 1) * S], b.ap[:, S:2 * S], ACT.Sigmoid, bias=pv("lru_bx", h))
            b.free = [a]
            yield
        g2_last[q] = m
        for j in range(4):
            c = slice(j * S, (j + 1) * S)
            a = act(T4[:, c], R4[:, c], ACT.Tanh, a, sp_tok, *ls_free, scale=SP[:, 4 * q + j:4 * q + j + 1])
        vi = tt(I4, I4, Y[:, 4 * q:4 * q + 4, :].rearrange("p a n -> p (a n)"), ALU.mult, a)
        yield
        for j in range(4):
            c = slice(j * S, (j + 1) * S)
            a = act(A4[:, c], R4[:, c], ACT.Exp, scale=SN[:, 4 * q + j:4 * q + j + 1])
        yield
        v = tt(R4, A4, A4, ALU.mult, a)
        yield
        v = stt(T4, R4, 1.0, T4, ALU.add, ALU.mult, v)
        yield
        a = act(T4, T4, ACT.Sqrt, v)
        yield
        v = tt(I4, T4, I4, ALU.mult, a, vi)
        yield
        for j in range(4):
            h = 4 * q + j
            c = slice(j * S, (j + 1) * S)
            y_tok[h] = Q.op("dve", lambda e, h=h, c=c: e.tensor_tensor_scan(Y[:, h, :], A4[:, c], I4[:, c], 0.0,
                                                                           ALU.mult, ALU.add), v, m)
        ls_free[:] = ri_free[q % 2] = [y_tok[4 * q + 3]]
        yield

    g2_last = [None] * 4
    for h in range(16):
        b = gemm(XA, ALLK, None)
        s = UP.next()
        v = evac(b, s.ap[:, 3:3 + S], *s.free, bias=pv("b_in", h))
        w = [pv("conv_w", k * 16 + h) for k in range(4)]
        v = ts(Y[:, h, :], s.ap[:, 0:S], w[0], pv("conv_b", h), ALU.mult, ALU.add, v, *g1_free)
        for k in range(1, 4):
            v = stt(Y[:, h, :], s.ap[:, k:k + S], w[k], Y[:, h, :], ALU.mult, ALU.add, v)
        s.free = [v]
        uc_tok[h] = v
        if h % 4 == 3:
            first.append(lru_batch(h // 4))

    kT = G3[:, 0:1024].rearrange("p (g n) -> p g n", g=4)
    vtok = G3[:, 1024:2048].rearrange("p (b n) -> p b n", b=2)
    mask = G3[:, 2048:2304]
    mask_tok = load(mask, d["mask"], *g3_free)
    PB = Turns([G3[:, 2304 + 384 * i:2688 + 384 * i] for i in range(2)])
    PT = Turns([G3[:, 3072 + 384 * i:3456 + 384 * i] for i in range(2)])
    ST = Turns([G3[:, 3840 + 8 * i:3848 + 8 * i] for i in range(3)])
    kv_tok = {}

    def v_turn(src, s, tv, dst, key):
        b = MB.next()
        for tb in range(2):
            m = turn(b.ap[:, tb * P:(tb + 1) * P], src[:, tb * P:(tb + 1) * P], tv, id_tok, *b.free)
        s.free = [m]
        a = act(dst, b.ap[:, 0:S].rearrange("p (b n) -> p b n", b=2), ACT.Copy, m)
        b.free = [a]
        kv_tok[key] = a
        yield

    for o in range(8):
        b = gemm(XA, ALLK, None)
        g = o % 4
        if o < 4:
            kv_tok["k", g] = evac(b, kT[:, g, :], *g3_free, bias=pv("b_in", 48 + o))
        else:
            s = TT.next()
            v = evac(b, s.ap, *s.free, *g3_free, bias=pv("b_in", 48 + o))
            for _ in v_turn(s.ap, s, v, vtok[:, :, g * P:(g + 1) * P], ("v", g)):
                pass
    QT = G2[:, :].rearrange("p (h n) -> p h n", h=16)
    q_tok = [None] * 16
    o_tok = [None] * 16
    SCALE = float(P) ** -0.5

    def head(h):
        g = h // 4
        b = MB.next()
        mm(b.ap[:, 0:P], QT[:, h, 0:P], kT[:, g, 0:P], True, True, q_tok[h], kv_tok["k", g], *b.free)
        m = mm(b.ap[:, P:P + S], QT[:, h, P:2 * P], kT[:, g, :], True, True)
        pb, st = PB.next(), ST.next()
        p = pb.ap
        v = stt(p[:, 0:P], b.ap[:, 0:P], SCALE, mask[:, P:2 * P], ALU.mult, ALU.add, m, mask_tok, *pb.free)
        v2 = stt(p[:, P:P + S], b.ap[:, P:P + S], SCALE, mask, ALU.mult, ALU.add)
        b.free = [v2]
        x = st.ap
        v = vmax(x[:, 0:1], p[:, 0:P], v, *st.free)
        v = vmax(x[:, 1:2], p[:, P:P + S], v2)
        v = ts(x[:, 0:2], x[:, 0:2], pv("sinks", h), -1.0, ALU.max, ALU.mult, v)
        yield
        a = act(p[:, 0:P], p[:, 0:P], ACT.Exp, v, bias=x[:, 0:1], accum_out=x[:, 2:3])
        a = act(p[:, P:P + S], p[:, P:P + S], ACT.Exp, bias=x[:, 1:2], accum_out=x[:, 3:4])
        a = act(x[:, 4:6], x[:, 0:2], ACT.Exp, bias=pv("sinks", h))
        yield
        v = tt(x[:, 2:4], x[:, 2:4], x[:, 4:6], ALU.add, a)
        v = recip(x[:, 2:4], x[:, 2:4], v)
        v1 = ts(p[:, 0:P], p[:, 0:P], x[:, 2:3], None, ALU.mult, None, v)
        v = ts(p[:, P:P + S], p[:, P:P + S], x[:, 3:4], None, ALU.mult, None)
        st.free = [v]
        yield
        b = MB.next()
        turn(b.ap[:, 0:P], p[:, 0:P], v, *b.free)
        turn(b.ap[:, P:2 * P], p[:, P:2 * P])
        m = turn(b.ap[:, 2 * P:3 * P], p[:, 2 * P:3 * P])
        pb.free = [m]
        pt = PT.next()
        a = act(pt.ap, b.ap[:, 0:384], ACT.Copy, m, *pt.free)
        b.free = [a]
        yield
        b = MB.next()
        v0, v1_ = vtok[:, 0, g * P:(g + 1) * P], vtok[:, 1, g * P:(g + 1) * P]
        mm(b.ap[:, 0:P], v0, pt.ap[:, 0:P], True, True, a, kv_tok["v", g], *b.free)
        mm(b.ap[:, P:2 * P], v0, pt.ap[:, P:2 * P], True, False)
        m = mm(b.ap[:, P:2 * P], v1_, pt.ap[:, 2 * P:3 * P], False, True)
        pt.free = [m]
        o_tok[h] = act(QT[:, h, :], b.ap[:, 0:S], ACT.Copy, m)
        b.free = [o_tok[h]]
        yield

    while g2_last[3] is None:
        background()
    for o in range(16):
        b = gemm(XA, ALLK, None)
        q_tok[o] = evac(b, QT[:, o, :], g2_last[3], bias=pv("b_in", 32 + o))
        later(head(o))
    while first:
        background()

    yl_ready = [None] * KT
    lru_last = y_tok[15]
    for o in range(16):
        b = gemm(XA, ALLK, None)
        s = TT.next()
        v = evac(b, s.ap, *s.free, bias=pv("b_in", 16 + o))
        a = act(s.ap, s.ap, ACT.Gelu_apprx_tanh, v)
        v = tt(s.ap, s.ap, Y[:, o, :], ALU.mult, a, y_tok[o])
        split_later(XB, o, s.ap, s, yl_ready, v, lru_last)

    M = G1
    m_tok = [None] * KT
    for o in range(16):
        bm = gemm(XA, ALLK, None)
        s = TT.next()
        v = evac(bm, s.ap, *s.free, bias=pv("b_in", 56 + o))
        a = act(s.ap, s.ap, ACT.Sigmoid, v)
        bl = gemm(XB, ALLK, yl_ready)
        s2 = EV.next()
        v = evac(bl, s2.ap, *s2.free)
        m_tok[o] = tt(M[:, o, :], s.ap, s2.ap, ALU.mult, v, a)
        s.free = s2.free = [m_tok[o]]
    drain_background()
    xb_pe = pe_last[0]

    ya_ready = [None] * KT
    gate_tok = [None] * KT
    for o in range(16):
        split_later(XB, o, QT[:, o, :], None, ya_ready, o_tok[o], xb_pe)
        b = gemm(XA, ALLK, None)
        v = evac(b, QT[:, o, :], ya_ready[o], bias=pv("b_in", 72 + o))
        gate_tok[o] = act(QT[:, o, :], QT[:, o, :], ACT.Sigmoid, v)
    xa_pe = pe_last[0]
    mg_ready = [None] * KT
    for o in range(16):
        b = gemm(XB, ALLK, ya_ready)
        s = TT.next()
        v = evac(b, s.ap, *s.free)
        v = tt(s.ap, s.ap, QT[:, o, :], ALU.mult, v, gate_tok[o])
        v = tt(s.ap, s.ap, M[:, o, :], ALU.add, v, m_tok[o])
        split_later(XA, o, s.ap, s, mg_ready, v, xa_pe)

    def residual(o, b, gate, first_w):
        s = TT.next()
        v = evac(b, s.ap, *s.free, *first_w, scale=gate)
        res_tok[o] = tt(RES[:, o, :], RES[:, o, :], s.ap, ALU.add, v, res_tok[o])
        s.free = [res_tok[o]]

    s2_ = Sum(SA[:, :], s1.done)
    for o in range(16):
        if o == 12:
            root_table()
        b = gemm(XA, ALLK, mg_ready)
        residual(o, b, MOD[:, 32 + o:33 + o], [mod_tok[4], mod_tok[5]])
        s2_.add_later(RES[:, o, :], res_tok[o])
    soon_all()
    xa_pe = pe_last[0]
    sc_tok = scale_of("norm2_g", 64)
    inv_tok = s2_.inv(INV[:, :], DM, h_last)
    norm2_last = ramp(XA, ALLK, modulated(XA, 48, sc_tok, inv_tok, xa_pe))

    f_last = [pe_last[0]]

    sF = Sum(SA[:, :], s2_.done)
    sG = Sum(G2[:, S:2 * S], gate_tok[15], mg_ready[15])
    for ci, ch in enumerate(CHUNKS):
        f_ready = [None] * KT
        for j, hh in enumerate(ch):
            bg_ = gemm(XA, ALLK, None)
            s = TT.next()
            v = evac(bg_, s.ap, *s.free)
            a = act(s.ap, s.ap, ACT.Silu, v)
            bu = gemm(XA, ALLK, None)
            s2 = EV.next()
            v = evac(bu, s2.ap, *s2.free)
            v = tt(s.ap, s.ap, s2.ap, ALU.mult, v, a)
            s2.free = [v]
            split_later(XB, j, s.ap, s, f_ready, v, f_last[0])
        for o in range(16):
            if o == 12 and ci == len(CHUNKS) - 1:
                root_table()
            b = gemm(XB, list(range(len(ch))), f_ready)
            residual(o, b, MOD[:, 80 + o:81 + o], [mod_tok[10], mod_tok[11]])
            if ci == len(CHUNKS) - 1:
                sF.add_later(RES[:, o, :], res_tok[o])
                sG.add_later(RES[:, o, :], res_tok[o], scale=pv("final_g", o))
        f_last[0] = pe_last[0]
    xa_pe = pe_last[0]

    soon_all()
    bF, bG = MB.next(), MB.next()
    mF = mm(bF.ap[:, 0:S], ONE[:, :], sF.acc, True, True, sF.last, *bF.free)
    mG = mm(bG.ap[:, 0:S], ONE[:, :], sG.acc, True, True, sG.last, *bG.free)
    sF.done = mF
    t2 = G2[:, 768:1024]
    v = ts(t2, bF.ap[:, 0:S], EPS / DM, EPS * EPS, ALU.mult, ALU.add, mF)
    v = stt(t2, bG.ap[:, 0:S], 1.0 / DM, t2, ALU.mult, ALU.add, mG, v)
    bG.free = [v]
    a = act(t2, t2, ACT.Sqrt, v)
    inv2_tok = recip(t2, t2, a)
    inv_act = act(INV[:, :], bF.ap[:, 0:S], ACT.Sqrt, norm2_last, scale=1.0 / DM, bias=SM[:, 112:113])
    bF.free = [inv_act]
    FG = SM[:, 0:16]
    fg_tok = tt(FG, pv("final_g", 0, 16), pv("pre_mix_gain_2", 0, 16), ALU.mult)
    inv_tok = []

    def normed(kt):
        end = scaled(XA, kt, RES[:, kt, :], res_tok[kt], t2, [inv2_tok, fg_tok], FG[:, kt:kt + 1], xa_pe)

        def both():
            v = end()
            if kt == 0:
                inv_tok.append(recip(INV[:, :], INV[:, :], inv_act))
            res_tok[kt] = stt(RES[:, kt, :], RES[:, kt, :], pv("final_g", kt), INV[:, :], ALU.mult, ALU.mult,
                              inv_tok, sG.last)
            return v
        return both

    UT = G1[:, 0:8, :]
    X0 = G1[:, 8:16, :]
    g1_done = [mg_ready[15]]
    g3_done = [o_tok[15]]
    xb_done = [f_last[0]]
    QN = G2[:, 0:2048].rearrange("p (h n) -> p h n", h=8)
    KN = G2[:, 2048:4096].rearrange("p (h n) -> p h n", h=8)
    utok = G3[:, 0:2048].rearrange("p (b n) -> p b n", b=2)
    kpz = G3[:, 3352:3864].rearrange("p (a n) -> p a n", a=2)
    sk_acc = G3[:, 3864:4120]
    vt2 = ACC[:, :, :]
    QP = XBf[:, 3072:4096].rearrange("p (a n) -> p a n", a=4)
    cq = XBf[:, 4096:5632].rearrange("p (a n) -> p a n", a=6)
    rope = XBf[:, 5632:6144].rearrange("p (a n) -> p a n", a=2)
    r1, r2, sk_inv = XBf[:, 6144:6400], XBf[:, 6400:6656], XBf[:, 6656:6912]
    rope_tok = load(rope, d["rope"], *xb_done)

    def conv_buffers(at_, *w):
        ins = Turns([at_[:, 264 * i:264 * i + 258] for i in range(3)])
        outs = Turns([at_[:, 792 + S * i:792 + S * (i + 1)] for i in range(2)])
        for s in ins.slots:
            memset(s.ap[:, 0:1], 0.0, *w)
            s.free = [memset(s.ap[:, 257:258], 0.0, *w)]
        for s in outs.slots:
            s.free = list(w)
        return ins, outs

    def conv3(b, ins, o, wname, bname, j, n, *w, by=None, by_tok=None):
        s = ins.next()
        v = evac(b, s.ap[:, 1:1 + S], *s.free)
        if by is not None:
            v = tt(s.ap[:, 1:1 + S], s.ap[:, 1:1 + S], by, ALU.mult, v, by_tok)
        v = ts(o, s.ap[:, 0:S], pv(wname, j), pv(bname, j), ALU.mult, ALU.add, v, *w)
        for k in (1, 2):
            v = stt(o, s.ap[:, k:k + S], pv(wname, k * n + j), o, ALU.mult, ALU.add, v)
        s.free = [v]
        return v

    cq_tok = [None] * 6
    sQ, sK = Sum(SA[:, :], sF.done), Sum(sk_acc, *g3_done)
    xn_last = ramp(XA, ALLK, normed)
    conv_in, conv_out = conv_buffers(G3[:, 2048:3352], *g3_done)
    for o in range(8):
        b = gemm(XA, ALLK, None)
        if o < 6:
            cq_tok[o] = evac(b, cq[:, o, :], *xb_done)
            (sQ if o < 4 else sK).add_later(cq[:, o, :], cq_tok[o])
        elif o == 6:
            soon_all()
            invq = sQ.inv(INV[:, :], 512, res_tok[15])
            invk = sK.inv(sk_inv, 256, *xb_done)
            v = evac(b, r1, *xb_done)
            ka = tt(r1, r1, rope[:, 0, :], ALU.mult, v, rope_tok)
        else:
            v = evac(b, r2, *xb_done)
            kb = tt(r2, r2, rope[:, 1, :], ALU.mult, v)

    c_ready = [None] * 6
    kp_tok = []

    def small_sides():
        for k in (4, 5, 0, 1, 2, 3):
            inv, it = (INV[:, :], invq) if k < 4 else (sk_inv, invk)
            gain = pv("q_norm_gain_2", k) if k < 4 else pv("kv_norm_gain_2", k - 4)
            end = scaled(XB, k, cq[:, k, :], cq_tok[k], inv, it, gain, *xb_done)
            yield
            c_ready[k] = end()
        v = memset(kpz, 0.0, *g3_done)
        tt(kpz[0:64, 0, :], r1[0:64, :], r2[0:64, :], ALU.add, v, ka, kb)
        kp_tok.append(tt(kpz[64:128, 1, :], r1[64:128, :], r2[64:128, :], ALU.add))

    ut_tok = [None] * 8
    x0_tok = [None] * 8
    utok_tok = [None] * 8

    def u_turn(j):
        b = MB.next()
        for tb in range(2):
            m = turn(b.ap[:, tb * P:(tb + 1) * P], UT[:, j, tb * P:(tb + 1) * P], ut_tok[j], *b.free)
        a = act(utok[:, :, j * P:(j + 1) * P], b.ap[:, 0:S].rearrange("p (b n) -> p b n", b=2), ACT.Copy, m, *g3_done)
        b.free = [a]
        utok_tok[j] = a

    def hyena(j):
        b = gemm(XA, ALLK, None)
        if j:
            u_turn(j - 1)
        c1 = conv_out.next()
        va = conv3(b, conv_in, c1.ap, "hyena_conv_w_2", "hyena_conv_b_2", 8 + j, 24, *c1.free)
        b = gemm(XA, ALLK, None)
        vb = conv3(b, conv_in, UT[:, j, :], "hyena_conv_w_2", "hyena_conv_b_2", 16 + j, 24, *g1_done)
        ut_tok[j] = tt(UT[:, j, :], UT[:, j, :], c1.ap, ALU.mult, va, vb)
        c1.free = [ut_tok[j]]

    soon.append(small_sides())
    hyena(0)
    hyena(1)
    while not kp_tok:
        soon_step()
    width[0] = 3

    kn_tok, v2_tok, qn_tok, qp_tok = {}, {}, {}, {}
    for h in range(8):
        b = gemm(XB, [4, 5], c_ready)
        kn_tok[h] = evac(b, KN[:, h, :], xn_last)
    for h in range(8):
        b = gemm(XB, [4, 5], None)
        s = TT.next()
        v = evac(b, s.ap, *s.free)
        if h:
            v_last()

        def v_last(h=h, s=s, v=v):
            bt = MB.next()
            for tb in range(2):
                m = turn(bt.ap[:, tb * P:(tb + 1) * P], s.ap[:, tb * P:(tb + 1) * P], v, *bt.free)
            s.free = [m]
            v2_tok[h] = act(vt2[:, :, h * P:(h + 1) * P], bt.ap[:, 0:S].rearrange("p (b n) -> p b n", b=2), ACT.Copy, m,
                            mod_tok[10], mod_tok[11])
            bt.free = [v2_tok[h]]

    PB2 = Turns([XBf[:, 512 * i:512 * (i + 1)] for i in range(3)])
    PT2 = Turns([XBf[:, 1536 + 512 * i:2048 + 512 * i] for i in range(3)])
    ST2 = Turns([G3[:, 4120 + 8 * i:4128 + 8 * i] for i in range(3)])
    SC2 = float(192) ** -0.5
    oa_tok = [None] * 8
    heads = {"left": 8}

    def head2(h):
        b = MB.next()
        for qb in range(2):
            q = slice(qb * P, (qb + 1) * P)
            mm(b.ap[:, qb * S:(qb + 1) * S], QN[:, h, q], KN[:, h, :], True, False, qn_tok[h], kn_tok[h], *b.free)
            m = mm(b.ap[:, qb * S:(qb + 1) * S], QP[:, h // 2, q], kpz[:, h % 2, :], False, True,
                   qp_tok[h // 2], kp_tok)
        pb, st = PB2.next(), ST2.next()
        p, x = pb.ap, st.ap
        v = vmax(x[:, 0:2], b.ap.rearrange("p (b n) -> p b n", b=2), m, *st.free)
        v = ts(x[:, 0:2], x[:, 0:2], -SC2, None, ALU.mult, None, v)
        yield
        for qb in range(2):
            a = act(p[:, qb * S:(qb + 1) * S], b.ap[:, qb * S:(qb + 1) * S], ACT.Exp, v, *pb.free,
                    bias=x[:, qb:qb + 1], scale=SC2, accum_out=x[:, 2 + qb:3 + qb])
        b.free = [a]
        yield
        v = recip(x[:, 2:4], x[:, 2:4], a)
        for qb in range(2):
            v1 = ts(p[:, qb * S:(qb + 1) * S], p[:, qb * S:(qb + 1) * S], x[:, 2 + qb:3 + qb], None, ALU.mult, None, v)
        st.free = [v1]
        yield
        b = MB.next()
        for kb in range(2):
            for qb in range(2):
                m = turn(b.ap[:, kb * S + qb * P:kb * S + qb * P + P], p[:, qb * S + kb * P:qb * S + kb * P + P],
                         v1, *b.free)
        pb.free = [m]
        pt = PT2.next()
        a = act(pt.ap, b.ap, ACT.Copy, m, *pt.free)
        b.free = [a]
        yield
        b = MB.next()
        for kb in range(2):
            m = mm(b.ap[:, 0:S], vt2[:, kb, h * P:(h + 1) * P], pt.ap[:, kb * S:(kb + 1) * S], kb == 0, kb == 1,
                   a, v2_tok[h], *b.free)
        pt.free = [m]
        oa_tok[h] = act(QN[:, h, :], b.ap[:, 0:S], ACT.Copy, m)
        b.free = [oa_tok[h]]
        heads["left"] -= 1
        heads["pe"] = m

    for h in range(8):
        b = gemm(XB, [0, 1, 2, 3], None)
        qn_tok[h] = evac(b, QN[:, h, :], xn_last)
        if h == 0:
            v_last()
    for t in range(4):
        b = gemm(XB, [0, 1, 2, 3], None)
        s = TT.next()
        v = evac(b, s.ap, *s.free)
        v = tt(QP[:, t, :], s.ap, rope[:, 0, :], ALU.mult, v, *xb_done)
        b = gemm(XB, [0, 1, 2, 3], None)
        v2 = evac(b, s.ap, v)
        v2 = tt(s.ap, s.ap, rope[:, 1, :], ALU.mult, v2)
        qp_tok[t] = tt(QP[:, t, :], QP[:, t, :], s.ap, ALU.add, v2, v)
        s.free = [qp_tok[t]]
    c_pe = pe_last[0]
    for s in PB2.slots + PT2.slots:
        s.free = [c_pe]
    for h in range(8):
        later(head2(h))
    KF = XBf[:, 4096:8192].rearrange("p (a f n) -> p a f n", a=2, f=2)
    kf_tok = load(XBf[:, 4096:8192], kf_dram, g1_free[0], qp_tok[3], kp_tok[0])
    for j in range(2, 8):
        hyena(j)
    drain_background()

    UF = XBf[:, 0:4096].rearrange("p (a f n) -> p a f n", a=2, f=2)
    dft_b = G2[:, 2048:3072].rearrange("p (a b f) -> p a b f", a=2, b=2)
    idft_b = G2[:, 3072:4096].rearrange("p (a b f) -> p a b f", a=2, b=2)
    dft_tok = load(dft_b, d["dft"], heads["pe"])
    idft_tok = load(idft_b, d["idft"], heads["pe"])
    prod = ACC[:, :, 0:512]
    io = G3[:, 3352:3608]
    uf_tok = {}
    last = {"prod": None}
    yh_tok = [None] * 8
    sY, sO = Sum(SA[:, :], sQ.done), Sum(sk_acc, sK.done)

    def spectrum():
        for ch in range(2):
            c = slice(ch * 512, (ch + 1) * 512)
            for f in range(2):
                for a_ in range(2):
                    b = MB.next()
                    for tb in range(2):
                        m = mm(b.ap, dft_b[:, a_, tb, f * P:(f + 1) * P], utok[:, tb, c],
                               tb == 0, tb == 1, dft_tok, *utok_tok[4 * ch:4 * ch + 4], *b.free)
                    a = act(UF[:, a_, f, c], b.ap, ACT.Copy, m, heads["pe"])
                    b.free = [a]
                yield
                ur, vv, kr, ki = UF[:, 0, f, c], UF[:, 1, f, c], KF[:, 0, f, c], KF[:, 1, f, c]
                v1 = tt(prod[:, 0, :], ur, ki, ALU.mult, a, kf_tok, heads["pe"])
                v2 = tt(prod[:, 1, :], vv, ki, ALU.mult)
                v3 = tt(ur, ur, kr, ALU.mult, v1)
                v4 = tt(vv, vv, kr, ALU.mult, v2)
                tt(ur, ur, prod[:, 1, :], ALU.add, v3, v2)
                v6 = tt(vv, prod[:, 0, :], vv, ALU.subtract, v4)
                last["prod"] = v6
                uf_tok[f, ch] = v6

    def inverse(j):
        b = MB.next()
        n = 0
        for a_ in range(2):
            for f in range(2):
                m = mm(b.ap[:, 0:S], UF[:, a_, f, j * P:(j + 1) * P], idft_b[:, a_, f, :], n == 0, n == 3,
                       uf_tok[f, j // 4], idft_tok, *b.free)
                n += 1
        v = stt(UT[:, j, :], UT[:, j, :], pv("hyena_bias_2", j), b.ap[:, 0:S], ALU.mult, ALU.add, m, utok_tok[j])
        b.free = [v]
        last["uf"] = m
        yh_tok[j] = v

    def by_x0(j):
        yh_tok[j] = tt(UT[:, j, :], UT[:, j, :], X0[:, j, :], ALU.mult, yh_tok[j], x0_tok[j])
        (sY.add_later if j == 7 else sY.add)(UT[:, j, :], yh_tok[j])

    u_turn(7)
    spec = spectrum()
    for j in range(8):
        if j < 7:
            sO.add_later(QN[:, j, :], oa_tok[j])
        if j == 6:
            sO.add_later(QN[:, 7, :], oa_tok[7])
            root_table()
        if j == 7:
            soon_all()
            invo = sO.inv(io, 1024, heads["pe"])
        b = gemm(XA, ALLK, None)
        x0_tok[j] = conv3(b, conv_in, X0[:, j, :], "hyena_conv_w_2", "hyena_conv_b_2", j, 24, *g1_done)
        next(spec, None)
        for i in {3: [0], 4: [1, 2], 5: [3, 4], 6: [5, 6], 7: [7]}.get(j, []):
            inverse(i)
            if i < 7:
                by_x0(i)
    xa_pe = pe_last[0]

    invy = []

    def branch(kt):
        if kt == 9:
            by_x0(7)
        if kt == 13:
            soon_all()
            invy.append(sY.inv(INV[:, :], 1024, c_ready[3]))
        if kt < 8:
            return scaled(XA, kt, UT[:, kt, :], yh_tok[kt], INV[:, :], invy, pv("hyena_out_gain_2", kt), xa_pe)
        return scaled(XA, kt, QN[:, kt - 8, :], oa_tok[kt - 8], io, invo, pv("attn_out_gain_2", kt - 8), xa_pe)

    MX = G1
    mx_tok = [None] * KT
    mx_last = ramp(XA, [*range(8, 16), *range(8)], branch)
    sM = Sum(SA[:, :], sY.done)
    for o in range(16):
        b = gemm(XA, [*range(8, 16), *range(8)], None)
        mx_tok[o] = evac(b, MX[:, o, :], mx_last)
        sM.add_later(MX[:, o, :], mx_tok[o])
        if o == 12:
            root_table()
    soon_all()
    mx_pe = pe_last[0]
    invm = sM.inv(INV[:, :], DM, mx_last)

    bH = MB.next()
    INV2 = G3[:, 3352:3608]

    def mixed(kt):
        s = TT.next()
        v = stt(s.ap, MX[:, kt, :], pv("post_mix_gain_2", kt), INV[:, :], ALU.mult, ALU.mult, invm, mx_tok[kt], *s.free)
        res_tok[kt] = tt(RES[:, kt, :], RES[:, kt, :], s.ap, ALU.add, v, res_tok[kt])
        a = act(XA[kt][:, 0:S], RES[:, kt, :], ACT.Identity, res_tok[kt], mx_pe, scale=pv("pre_ffn_gain_2", kt))
        sq = act(s.ap, RES[:, kt, :], ACT.Square, res_tok[kt])

        def end():
            v = stt(XA[kt][:, S:2 * S], RES[:, kt, :], pv("pre_ffn_gain_2", kt), XA[kt][:, 0:S].bitcast(F32),
                    ALU.mult, ALU.subtract, a)
            m = mm(bH.ap[:, 0:S], ONE[:, :], s.ap, kt == 0, kt == KT - 1, sq, *(bH.free if kt == 0 else []))
            s.free = [m]
            mixed_sum[0] = m
            return v
        return end

    mixed_sum = [None]
    mixed_last = ramp(XA, ALLK, mixed)
    a = act(INV2, bH.ap[:, 0:S], ACT.Sqrt, mixed_sum[0], mx_last, scale=1.0 / DM, bias=SM[:, 112:113])
    bH.free = [a]
    invh = recip(INV2, INV2, a)

    FA = G2[:, :].rearrange("p (k n) -> p k n", k=KT)
    fa_tok = [mx_last] * KT
    f_last = [mx_pe]
    conv_in, conv_out = conv_buffers(G3[:, 0:1304], mx_last, mx_pe)
    sE = Sum(SA[:, :], sM.done)
    for ci, ch in enumerate(CHUNKS):
        f_ready = [None] * KT
        for j, hh in enumerate(ch):
            b = gemm(XA, ALLK, None)
            s = conv_out.next()
            v = conv3(b, conv_in, s.ap, "ffn_conv_w_2", "ffn_conv_b_2", hh, NHID, *s.free, by=INV2, by_tok=invh)
            a = act(s.ap, s.ap, ACT.Gelu_apprx_tanh, v)
            b = gemm(XA, ALLK, None)
            s2 = EV.next()
            v = evac(b, s2.ap, *s2.free)
            v2 = tt(s2.ap, s2.ap, INV2, ALU.mult, v)
            v = tt(s.ap, s.ap, s2.ap, ALU.mult, v2, a)
            s2.free = [v]
            split_later(XB, j, s.ap, s, f_ready, v, f_last[0])
        for o in range(16):
            if o == 12 and ci == len(CHUNKS) - 1:
                root_table()
            b = gemm(XB, list(range(len(ch))), f_ready)
            if ci == 0:
                fa_tok[o] = evac(b, FA[:, o, :], fa_tok[o])
            else:
                s = TT.next()
                v = evac(b, s.ap, *s.free)
                fa_tok[o] = tt(FA[:, o, :], FA[:, o, :], s.ap, ALU.add, v, fa_tok[o])
                s.free = [fa_tok[o]]
            if ci == len(CHUNKS) - 1:
                sE.add_later(FA[:, o, :], fa_tok[o])
        f_last[0] = pe_last[0]

    OUT = G1[:, :, :].rearrange("p a n -> p (a n)").rearrange("p (b n) -> p b n", b=2)
    banks = []

    def turn_res(g):
        turns = GB if g < 2 else MB
        bs = [turns.next(), turns.next()]
        for i in range(4):
            for tb in range(2):
                mm(bs[tb].ap[:, i * P:(i + 1) * P], RES[:, 4 * g + i, tb * P:(tb + 1) * P], IDN[:, :], i == 0, False,
                   *bs[tb].free)
        banks.append(bs)

    soon_all()
    turn_res(0)
    turn_res(1)
    inve = sE.inv(INV[:, :], DM, mixed_last)
    turn_res(2)
    turn_res(3)
    for g in range(4):
        bs = banks[g]
        for i in range(4):
            kt = 4 * g + i
            v = stt(FA[:, kt, :], FA[:, kt, :], pv("post_ffn_gain_2", kt), INV[:, :], ALU.mult, ALU.mult, inve, fa_tok[kt])
            for tb in range(2):
                m = mm(bs[tb].ap[:, i * P:(i + 1) * P], FA[:, kt, tb * P:(tb + 1) * P], IDN[:, :], False, True, v)
        for tb in range(2):
            a = act(OUT[:, tb, g * 512:(g + 1) * 512], bs[tb].ap, ACT.Copy, m, res_tok[15])
            bs[tb].free = [a]
        store(out[:, :, g * 512:(g + 1) * 512], OUT[:, :, g * 512:(g + 1) * 512], a)
    assert at["ring"] == len(plan) and at["sub"] == SUB and at["unit"] + 1 == at["split"], at
    Q.wait("pool", *stores)

    Q.count()
    block = ctx.enter_context(nc.Block())
    block.sync(lambda e: Q.emit("sp", e))
    block.scalar(lambda e: Q.emit("act", e))
    block.vector(lambda e: Q.emit("dve", e))
    block.gpsimd(lambda e: Q.emit("pool", e))
    block.tensor(lambda e: Q.emit("pe", e))


def tiled(w):
    k, n = w.shape
    return np.ascontiguousarray(w.reshape(k // P, P, n // P, P).transpose(2, 1, 0, 3)).reshape(n // P, P, k)


def tiled_parts(w):
    k, n = w.shape
    blocks = w.reshape(k // P, P, n // P, P).transpose(2, 0, 1, 3)
    tiles = []
    for c in CHUNKS:
        part = blocks[:, c.start:c.stop].reshape(-1, 16, P, P)
        tiles.append(part.transpose(0, 2, 1, 3).reshape(-1, P, 2048))
    return np.ascontiguousarray(np.concatenate(tiles))


def packed(blocks):
    return np.ascontiguousarray(np.stack(blocks).reshape(-1, 16, P, P).transpose(0, 2, 1, 3)).reshape(-1, P, 2048)


def blocks_of(w):
    return [w[i:i + P] for i in range(0, w.shape[0], P)]


def constants():
    f64 = np.float64
    n = 2 * S - 1
    t = np.arange(S, dtype=f64)
    f = np.arange(S, dtype=f64)
    ang = 2 * np.pi * ((t[:, None] * f[None, :]) % n) / n
    dft = np.stack([np.cos(ang), np.sin(ang)]).reshape(2, 2, P, S).transpose(2, 0, 1, 3)
    wf = np.where(f == 0, 1.0, 2.0)[:, None] / n
    idft = np.stack([wf * np.cos(ang.T), -wf * np.sin(ang.T)]).reshape(2, 2, P, S).transpose(2, 0, 1, 3)
    f32 = np.float32
    lin = np.linspace(0.0, 1.0, S).astype(f32)
    w = (2.0 * np.pi * np.arange(S) / S).astype(f32)
    fr = np.linspace(1e-4, 15, 16).astype(f32)
    a = (w[:, None] * fr[None, :]).astype(f32).astype(f64)
    z = np.concatenate([lin[:, None].astype(f64), np.cos(a), -np.sin(a)], axis=1)
    lo, hi = np.log(1e-2) / 1.5, np.log(1e-2) / 0.3
    deltas = np.abs(np.linspace(lo, hi, 1024)).astype(f32)
    win = np.exp(-(lin[:, None] * deltas[None, :]).astype(f64)) + 0.05
    window = win.reshape(2, P, 1024).transpose(1, 0, 2)
    inv = (1.0 / (f32(10000.0) ** (np.arange(0, 64, 2, dtype=f32) / f32(64)))).astype(f32)
    ra = (np.arange(S, dtype=f32)[:, None] * inv[None, :]).astype(f32).astype(f64)
    cos, sin = np.cos(ra).T, np.sin(ra).T
    rope = np.stack([np.concatenate([cos] * 4), np.concatenate([-sin, sin] * 2)]).transpose(1, 0, 2)
    q, k = np.arange(P)[:, None], np.arange(S)[None, :]
    mask = np.where((k > q) & (k <= q + P), 0.0, -1e30)
    out = {"dft": dft, "idft": idft, "zT": z.T, "window": window, "rope": rope, "mask": mask, "ident": np.eye(P)}
    return {k: np.ascontiguousarray(v.astype(f32)) for k, v in out.items()}


def ramped(tiles, columns):
    part = tiles[list(columns)].reshape(4, P, 16, P).transpose(2, 0, 1, 3)
    tiles[list(columns)] = part.reshape(4, 16, P, P).transpose(0, 2, 1, 3).reshape(4, P, 2048)


def layout(x):
    a = constants()
    cols = {}
    for name in PV:
        if name in ("sinks", "filt"):
            continue
        v = np.asarray(x[name], dtype=x[name].dtype)
        cols[name] = v.reshape(-1, P).T
    cols["sinks"] = np.broadcast_to(x["sinks"].reshape(1, 16), (P, 16))
    filt = [x[k].reshape(64) for k in ("filt_freq1_2", "filt_b1_2", "filt_freq2_2", "filt_b2_2")]
    pad = np.zeros(64, np.float32)
    cols["filt"] = np.stack([np.concatenate([v, pad]) for v in filt], axis=1)
    a["pv"] = np.ascontiguousarray(np.concatenate([cols[k] for k in PV], axis=1))
    a["x"] = np.ascontiguousarray(x["x"].reshape(2, P, DM).transpose(1, 0, 2))
    a["ada"] = np.ascontiguousarray(x["ada_w"].reshape(8, 2, P, 12, 1024).transpose(3, 0, 2, 1, 4)).reshape(12, 8, P, 2048)
    lw = np.stack([x["lru_wa"].reshape(16, P, P), x["lru_wx"].reshape(16, P, P)])
    a["lru_w"] = np.ascontiguousarray(lw.transpose(2, 0, 1, 3))
    for name in ("w_in", "w_lru_out", "w_attn_out", "w_o", "w_ffn_in"):
        a[name] = tiled(x[name][0])
    a["w_ffn_out"] = tiled_parts(x["w_ffn_out"][0])
    w = x["w_in_2"][0]
    pe = w[:, 3840:3904]
    rot = np.concatenate([pe[:, 32:], pe[:, :32]], axis=1)
    a["w_in2"] = tiled(np.concatenate([w[:, :3840], pe, pe, rot, rot], axis=1))
    ukv = x["w_ukv_2"][0].reshape(256, 8, 2, P)
    uq = x["w_uq_2"][0].reshape(512, 8, 192)
    blocks = []
    for part in range(2):
        for h in range(8):
            blocks += blocks_of(ukv[:, h, part])
    for h in range(8):
        blocks += blocks_of(uq[:, h, :P])
    for t in range(4):
        pes = [uq[:, 2 * t + i, P:] for i in range(2)]
        blocks += blocks_of(np.concatenate(pes, axis=1))
        blocks += blocks_of(np.concatenate([y for q in pes for y in (q[:, 32:], q[:, :32])], axis=1))
    a["w_u2"] = packed(blocks)
    w = x["w_out_2"][0]
    a["w_out2"] = tiled(np.concatenate([w[1024:], w[:1024]]))
    a["w_up2"] = tiled(x["w_up_2"][0])
    a["w_down2"] = tiled_parts(x["w_down_2"][0])
    for name, columns in RAMPS.items():
        ramped(a[name], columns)
    for name in ("filt_w1_2", "filt_w2_2", "filt_w3_2"):
        a[name] = np.ascontiguousarray(x[name][0])
    return a


def kernel(**inputs):
    import concourse.bacc as bacc
    from concourse.bass_utils import run_bass_kernel_spmd

    arrays = {f"in_{k}": v for k, v in layout({k: np.asarray(v) for k, v in inputs.items()}).items()}
    nc = bacc.Bacc("TRN2", target_bir_lowering=False, num_devices=1)
    d = {}
    for name, a in arrays.items():
        d[name[3:]] = nc.dram_tensor(name, a.shape, mybir.dt.from_np(a.dtype), kind="ExternalInput").ap()
    out = nc.dram_tensor("out", (1, S, DM), F32, kind="ExternalOutput").ap()
    program(nc, d, out.rearrange("a (b p) n -> p (a b) n", p=P))
    r = run_bass_kernel_spmd(nc, [arrays], core_ids=[0])
    return r.results[0]["out"]
```
